# Optimizing a Trainium2 kernel written in Bass

```python
import jax, jax.numpy as jnp
from jax import lax
import numpy as np
import jax
import jax.numpy as jnp

D_MODEL = 1024
BATCH = 1
SEQ = 256
DEPTH = 1

CHUNK = 64
N_HEADS = 8
HEAD_DIM = 64
ATTN_WIDTH = N_HEADS * HEAD_DIM
N_IDX_HEADS = 4
IDX_DIM = 64
TOPK_MAX = 256
Q_BLOCK = 128
POOL_WINDOWS = (2, 4, 8, 16)
N_POOL_GROUPS = 4
POOL_WIDTH = 512
POOL_GROUP = POOL_WIDTH // N_POOL_GROUPS
N_BRANCHES = 2
PEER_HEADS = 8
PEER_QDIM = 128
PEER_HALF = PEER_QDIM // 2
N_KEYS = 128
N_EXPERTS = N_KEYS * N_KEYS
PEER_TOPK = 16
TOKEN_BLOCK = 128
EPS = 1e-6
IN_SIZES = (ATTN_WIDTH, HEAD_DIM, HEAD_DIM, N_IDX_HEADS * IDX_DIM, IDX_DIM, N_IDX_HEADS, POOL_WIDTH, N_BRANCHES * D_MODEL)
IN_WIDTH = sum(IN_SIZES)


def rms_norm(x, g):
    x32 = x.astype(jnp.float32)
    y = x32 * lax.rsqrt(jnp.mean(x32 * x32, axis=-1, keepdims=True) + EPS)
    return (y * g.astype(jnp.float32)).astype(x.dtype)

def dsa_attention(q, k, v, iq, ik, iw):
    B, S = q.shape[0], q.shape[1]
    n_sel = min(TOPK_MAX, S // 4)
    n_blk = S // Q_BLOCK
    key_chunk = jnp.arange(S) // CHUNK
    idx_scale = IDX_DIM ** -0.5
    w_scale = N_IDX_HEADS ** -0.5
    attn_scale = HEAD_DIM ** -0.5

    def to_blocks(a):
        return jnp.swapaxes(a.reshape((B, n_blk, Q_BLOCK) + a.shape[2:]), 0, 1)

    def gather_rows(table, idx):
        return jax.vmap(lambda tb, ib: tb[ib])(table, idx)

    def one_block(args):
        qb, iqb, iwb, blk = args
        q_chunk = (blk * Q_BLOCK + jnp.arange(Q_BLOCK)) // CHUNK
        admissible = key_chunk[None, :] <= q_chunk[:, None]
        rel = jax.nn.relu(jnp.einsum('bqhd,bsd->bqhs', iqb, ik) * idx_scale)
        score = jnp.einsum('bqhs,bqh->bqs', rel, iwb * w_scale).astype(jnp.float32)
        score = jnp.where(admissible[None], score, -jnp.inf)
        _, sel = lax.top_k(score, n_sel)
        k_sel = gather_rows(k, sel)
        v_sel = gather_rows(v, sel)
        ok = key_chunk[sel] <= q_chunk[None, :, None]
        logits = jnp.einsum('bqhd,bqkd->bqhk', qb, k_sel).astype(jnp.float32) * attn_scale
        logits = jnp.where(ok[:, :, None, :], logits, -jnp.inf)
        p = jax.nn.softmax(logits, axis=-1).astype(v.dtype)
        return jnp.einsum('bqhk,bqkd->bqhd', p, v_sel)

    out = lax.map(one_block, (to_blocks(q), to_blocks(iq), to_blocks(iw), jnp.arange(n_blk)))
    return jnp.swapaxes(out, 0, 1).reshape(B, S, ATTN_WIDTH)

def pool_mixer(p, w_grp, s_pool):
    B, S = p.shape[0], p.shape[1]
    pg = p.reshape(B, S, N_POOL_GROUPS, POOL_GROUP).astype(jnp.float32)
    cs = jnp.pad(jnp.cumsum(pg, axis=1), ((0, 0), (1, 0), (0, 0), (0, 0)))
    t = jnp.arange(S)
    outs = []
    for g, w in enumerate(POOL_WINDOWS):
        cs_g = cs[:, :, g, :]
        lo = jnp.maximum(t + 1 - w, 0)
        cnt = (t + 1 - lo).astype(jnp.float32)
        mean = (cs_g[:, t + 1] - cs_g[:, lo]) / cnt[None, :, None]
        outs.append(mean - pg[:, :, g, :])
    mixed = jnp.stack(outs, axis=2).astype(p.dtype)
    mixed = jnp.einsum('bsgc,gcd->bsgd', mixed, w_grp) * s_pool
    return mixed.reshape(B, S, POOL_WIDTH)

def peer_ffn(h, w_q, sub_keys, u, v):
    B, S, D = h.shape
    n_blk = (B * S) // TOKEN_BLOCK
    hb = h.reshape(n_blk, TOKEN_BLOCK, D)

    def one_block(hx):
        q = (hx @ w_q).reshape(TOKEN_BLOCK, PEER_HEADS, 2, PEER_HALF)
        s = jnp.einsum('nhpd,hpkd->nhpk', q, sub_keys).astype(jnp.float32)
        top_s, top_i = lax.top_k(s, PEER_TOPK)
        cand = top_s[:, :, 0, :, None] + top_s[:, :, 1, None, :]
        best_s, best_p = lax.top_k(cand.reshape(TOKEN_BLOCK, PEER_HEADS, PEER_TOPK * PEER_TOPK), PEER_TOPK)
        i1 = jnp.take_along_axis(top_i[:, :, 0], best_p // PEER_TOPK, axis=-1)
        i2 = jnp.take_along_axis(top_i[:, :, 1], best_p % PEER_TOPK, axis=-1)
        expert = (i1 * N_KEYS + i2).reshape(TOKEN_BLOCK, PEER_HEADS * PEER_TOPK)
        gate = jax.nn.softmax(best_s, axis=-1).reshape(TOKEN_BLOCK, PEER_HEADS * PEER_TOPK).astype(hx.dtype)
        u_sel = u[expert]
        v_sel = v[expert]
        act = jax.nn.gelu(jnp.einsum('nd,ned->ne', hx, u_sel), approximate=False)
        return jnp.einsum('ne,ned->nd', gate * act, v_sel)

    return lax.map(one_block, hb).reshape(B, S, D)

def first_inputs(seed: int = 0) -> dict:
    key = jax.random.key(seed)
    ks = jax.random.split(key, 20)
    f32 = jnp.float32
    D = D_MODEL

    def nrm(k, shape, scale):
        return jax.random.normal(k, shape, f32) * scale

    return {
        'x': nrm(ks[0], (BATCH, SEQ, D), 1.0),
        'c': nrm(ks[1], (BATCH, D), 1.0),
        'w_ada': nrm(ks[2], (DEPTH, D, 6 * D), 0.5 * D ** -0.5),
        'b_ada': nrm(ks[3], (DEPTH, 6 * D), 0.02),
        'g_norm1': 1.0 + nrm(ks[4], (DEPTH, D), 0.02),
        'w_in': nrm(ks[5], (DEPTH, D, IN_WIDTH), D ** -0.5),
        'g_q': 1.0 + nrm(ks[6], (DEPTH, HEAD_DIM), 0.02),
        'g_k': 1.0 + nrm(ks[7], (DEPTH, HEAD_DIM), 0.02),
        'g_ik': 1.0 + nrm(ks[8], (DEPTH, IDX_DIM), 0.02),
        'w_pool_grp': nrm(ks[9], (DEPTH, N_POOL_GROUPS, POOL_GROUP, POOL_GROUP), POOL_GROUP ** -0.5),
        's_pool': 1.0 + nrm(ks[10], (DEPTH, N_POOL_GROUPS, POOL_GROUP), 0.1),
        'w_up_attn': nrm(ks[11], (DEPTH, ATTN_WIDTH, D), ATTN_WIDTH ** -0.5),
        'w_up_pool': nrm(ks[12], (DEPTH, POOL_WIDTH, D), POOL_WIDTH ** -0.5),
        'w_out': nrm(ks[13], (DEPTH, D, D), D ** -0.5),
        'g_norm2': 1.0 + nrm(ks[14], (DEPTH, D), 0.02),
        'w_peer_q': nrm(ks[15], (DEPTH, D, PEER_HEADS * PEER_QDIM), D ** -0.5),
        'peer_subkeys': nrm(ks[16], (DEPTH, PEER_HEADS, 2, N_KEYS, PEER_HALF), PEER_HALF ** -0.5),
        'peer_u': nrm(ks[17], (DEPTH, N_EXPERTS, D), D ** -0.5),
        'peer_v': nrm(ks[18], (DEPTH, N_EXPERTS, D), 0.5),
    }

def first_block(x, c, w_ada, b_ada, g_norm1, w_in, g_q, g_k, g_ik, w_pool_grp, s_pool,
              w_up_attn, w_up_pool, w_out, g_norm2, w_peer_q, peer_subkeys, peer_u, peer_v):
    B, S, D = x.shape
    cuts = [int(v) for v in np.cumsum(IN_SIZES)[:-1]]
    for layer in range(DEPTH):
        ada = c @ w_ada[layer] + b_ada[layer]
        shift1, scale1, gate1, shift2, scale2, gate2 = [a[:, None, :] for a in jnp.split(ada, 6, axis=-1)]

        h = rms_norm(x, g_norm1[layer]) * (1.0 + scale1) + shift1
        z = h @ w_in[layer]
        zq, zk, zv, ziq, zik, ziw, zp, zg = jnp.split(z, cuts, axis=-1)
        q = rms_norm(zq.reshape(B, S, N_HEADS, HEAD_DIM), g_q[layer])
        k = rms_norm(zk, g_k[layer])
        iq = ziq.reshape(B, S, N_IDX_HEADS, IDX_DIM)
        ik = rms_norm(zik, g_ik[layer])
        y_attn = dsa_attention(q, k, zv, iq, ik, ziw) @ w_up_attn[layer]
        y_pool = pool_mixer(zp, w_pool_grp[layer], s_pool[layer]) @ w_up_pool[layer]
        g_attn, g_pool = jnp.split(jax.nn.sigmoid(zg), 2, axis=-1)
        mixed = (g_attn * y_attn + g_pool * y_pool) @ w_out[layer]
        x = x + gate1 * mixed

        h2 = rms_norm(x, g_norm2[layer]) * (1.0 + scale2) + shift2
        x = x + gate2 * peer_ffn(h2, w_peer_q[layer], peer_subkeys[layer], peer_u[layer], peer_v[layer])
    return x


D_RNN = 1344
RNN_BLOCKS = 16
RNN_BLOCK_W = D_RNN // RNN_BLOCKS
RNN_CONV_W = 4
LRU_C = 8.0
N_HEADS_2 = 16
N_KV = 4
GROUP = N_HEADS_2 // N_KV
CMP_LEN = 32
CMP_STRIDE = 16
CMP_HIDDEN = 128
SEL_LEN = 64
N_SELECT = 16
WINDOW = 512
Q_BLOCK_2 = 64
D_FF = 3 * D_MODEL
FFN_CONV_W = 3
NEG = -1e30
FORCE = 1e6


def rms_norm_2(x, g):
    x32 = x.astype(jnp.float32)
    y = x32 * lax.rsqrt(jnp.mean(x32 * x32, axis=-1, keepdims=True) + EPS)
    return (y * g.astype(jnp.float32)).astype(x.dtype)

def causal_dwconv(x, w, b):
    k = w.shape[0]
    y = lax.conv_general_dilated(x, w[:, None, :].astype(x.dtype), window_strides=(1,),
                                 padding=[(k - 1, 0)], dimension_numbers=('NWC', 'WIO', 'NWC'),
                                 feature_group_count=x.shape[-1])
    return y + b.astype(x.dtype)

def masked_softmax(s, mask):
    p = jax.nn.softmax(jnp.where(mask, s, NEG), axis=-1)
    return p * mask

def rg_lru(x, w_a, b_a, w_x, b_x, lam):
    bsz, s, _ = x.shape
    xb = x.reshape(bsz, s, RNN_BLOCKS, RNN_BLOCK_W)
    r = jax.nn.sigmoid(jnp.einsum('bsnc,ncd->bsnd', xb, w_a).reshape(bsz, s, D_RNN) + b_a)
    i = jax.nn.sigmoid(jnp.einsum('bsnc,ncd->bsnd', xb, w_x).reshape(bsz, s, D_RNN) + b_x)
    log_a = LRU_C * r.astype(jnp.float32) * jax.nn.log_sigmoid(lam.astype(jnp.float32))
    a = jnp.exp(log_a)
    u = jnp.sqrt(-jnp.expm1(2.0 * log_a)) * (i * x).astype(jnp.float32)

    def combine(lhs, rhs):
        a1, b1 = lhs
        a2, b2 = rhs
        return a1 * a2, a2 * b1 + b2

    _, h = lax.associative_scan(combine, (a, u), axis=1)
    return h.astype(x.dtype)

def compress(kv, pe, w1, w2):
    bsz, s, g, hd = kv.shape
    nc = (s - CMP_LEN) // CMP_STRIDE + 1
    pos = np.arange(nc)[:, None] * CMP_STRIDE + np.arange(CMP_LEN)[None, :]
    blocks = kv[:, pos] + pe[None, None, :, None, :]
    blocks = blocks.transpose(0, 3, 1, 2, 4).reshape(bsz, g, nc, CMP_LEN * hd)
    return jax.nn.gelu(blocks @ w1) @ w2

def overlap_matrix(nc, ns):
    i = np.arange(nc)[:, None]
    j = np.arange(ns)[None, :]
    lo = np.maximum(i * CMP_STRIDE, j * SEL_LEN)
    hi = np.minimum(i * CMP_STRIDE + CMP_LEN, (j + 1) * SEL_LEN)
    return jnp.asarray(np.maximum(hi - lo, 0) / CMP_STRIDE, dtype=jnp.float32)

def nsa(q, kc, vc, ks, vs, kw, vw, gates, q_norm_g, k_cmp_norm_g, k_slc_norm_g, k_win_norm_g,
        cmp_pe_k, cmp_w1_k, cmp_w2_k, cmp_pe_v, cmp_w1_v, cmp_w2_v):
    bsz, s, _ = q.shape
    f32 = jnp.float32
    scale = HEAD_DIM ** -0.5

    def heads(t, n):
        return t.reshape(bsz, s, n, HEAD_DIM)

    qh = rms_norm_2(heads(q, N_HEADS_2), q_norm_g)
    qh = qh.reshape(bsz, s, N_KV, GROUP, HEAD_DIM).transpose(0, 2, 3, 1, 4)
    k_cmp = rms_norm_2(compress(heads(kc, N_KV), cmp_pe_k, cmp_w1_k, cmp_w2_k), k_cmp_norm_g)
    v_cmp = compress(heads(vc, N_KV), cmp_pe_v, cmp_w1_v, cmp_w2_v)
    nc = k_cmp.shape[2]
    ns = s // SEL_LEN
    k_slc = rms_norm_2(heads(ks, N_KV), k_slc_norm_g).transpose(0, 2, 1, 3).reshape(bsz, N_KV, ns, SEL_LEN, HEAD_DIM)
    v_slc = heads(vs, N_KV).transpose(0, 2, 1, 3).reshape(bsz, N_KV, ns, SEL_LEN, HEAD_DIM)
    pad = ((0, 0), (0, 0), (WINDOW, 0), (0, 0))
    k_win = jnp.pad(rms_norm_2(heads(kw, N_KV), k_win_norm_g).transpose(0, 2, 1, 3), pad)
    v_win = jnp.pad(heads(vw, N_KV).transpose(0, 2, 1, 3), pad)
    g = jax.nn.sigmoid(gates).reshape(bsz, s, N_KV, GROUP, 3).transpose(0, 2, 3, 1, 4)
    overlap = overlap_matrix(nc, ns)
    cmp_end = np.arange(nc) * CMP_STRIDE + CMP_LEN - 1
    n_top = min(N_SELECT, ns)
    gather = jax.vmap(jax.vmap(lambda blk, ix: blk[ix]))
    jb = jnp.arange(ns)

    def block(qi):
        st = qi * Q_BLOCK_2
        t = st + jnp.arange(Q_BLOCK_2)
        qb = lax.dynamic_slice_in_dim(qh, st, Q_BLOCK_2, axis=3)
        gb = lax.dynamic_slice_in_dim(g, st, Q_BLOCK_2, axis=3)
        sc = jnp.einsum('bgrqd,bgcd->bgrqc', qb, k_cmp).astype(f32) * scale
        p_cmp = masked_softmax(sc, cmp_end[None, :] <= t[:, None])
        o_cmp = jnp.einsum('bgrqc,bgcd->bgrqd', p_cmp.astype(v_cmp.dtype), v_cmp)
        imp = jnp.einsum('bgrqc,cn->bgqn', p_cmp, overlap)
        cur = t // SEL_LEN
        causal_b = jb[None, :] <= cur[:, None]
        forced = (jb[None, :] == 0) | (jb[None, :] == cur[:, None]) | (jb[None, :] == cur[:, None] - 1)
        rank = jnp.where(causal_b, jnp.where(forced, FORCE, imp), -FORCE)
        _, idx = lax.top_k(rank, n_top)
        kg = gather(k_slc, idx)
        vg = gather(v_slc, idx)
        kpos = idx[..., None] * SEL_LEN + jnp.arange(SEL_LEN)
        ok = (idx <= cur[:, None])[..., None] & (kpos <= t[:, None, None])
        sc = jnp.einsum('bgrqd,bgqnld->bgrqnl', qb, kg).astype(f32) * scale
        p = masked_softmax(sc.reshape(bsz, N_KV, GROUP, Q_BLOCK_2, n_top * SEL_LEN),
                           ok.reshape(bsz, N_KV, 1, Q_BLOCK_2, n_top * SEL_LEN))
        o_slc = jnp.einsum('bgrqm,bgqmd->bgrqd', p.astype(vg.dtype),
                           vg.reshape(bsz, N_KV, Q_BLOCK_2, n_top * SEL_LEN, HEAD_DIM))
        kwb = lax.dynamic_slice_in_dim(k_win, st, WINDOW + Q_BLOCK_2, axis=2)
        vwb = lax.dynamic_slice_in_dim(v_win, st, WINDOW + Q_BLOCK_2, axis=2)
        kp = st - WINDOW + jnp.arange(WINDOW + Q_BLOCK_2)
        okw = (kp[None, :] <= t[:, None]) & (kp[None, :] > t[:, None] - WINDOW) & (kp[None, :] >= 0)
        sc = jnp.einsum('bgrqd,bgkd->bgrqk', qb, kwb).astype(f32) * scale
        pw = masked_softmax(sc, okw)
        o_win = jnp.einsum('bgrqk,bgkd->bgrqd', pw.astype(vwb.dtype), vwb)
        return gb[..., 0:1] * o_cmp + gb[..., 1:2] * o_slc + gb[..., 2:3] * o_win

    out = lax.map(block, jnp.arange(s // Q_BLOCK_2))
    return out.transpose(1, 0, 4, 2, 3, 5).reshape(bsz, s, N_HEADS_2 * HEAD_DIM)

def second_inputs(seed: int = 0) -> dict:
    key = jax.random.key(seed)
    k = jax.random.split(key, 28)

    def nrm(kk, shape, scale):
        return jax.random.normal(kk, shape, jnp.float32) * scale

    d, hd = D_MODEL, HEAD_DIM
    n_in = 2 * D_RNN + N_HEADS_2 * hd + 6 * N_KV * hd + 3 * N_HEADS_2 + 2 * d
    u = jax.random.uniform(k[9], (D_RNN,), jnp.float32, 0.9, 0.999)
    sg = u ** (1.0 / LRU_C)
    lam = jnp.log(sg) - jnp.log1p(-sg)
    return {
        'x': nrm(k[0], (BATCH, SEQ, d), 1.0),
        'norm1_g': 1.0 + nrm(k[1], (d,), 0.02),
        'w_in': nrm(k[2], (d, n_in), d ** -0.5),
        'rnn_conv_w': nrm(k[3], (RNN_CONV_W, D_RNN), RNN_CONV_W ** -0.5),
        'rnn_conv_b': nrm(k[4], (D_RNN,), 0.02),
        'rg_w_a': nrm(k[5], (RNN_BLOCKS, RNN_BLOCK_W, RNN_BLOCK_W), RNN_BLOCK_W ** -0.5),
        'rg_b_a': nrm(k[6], (D_RNN,), 0.02),
        'rg_w_x': nrm(k[7], (RNN_BLOCKS, RNN_BLOCK_W, RNN_BLOCK_W), RNN_BLOCK_W ** -0.5),
        'rg_b_x': nrm(k[8], (D_RNN,), 0.02),
        'lru_lambda': lam,
        'w_rnn_out': nrm(k[10], (D_RNN, d), D_RNN ** -0.5),
        'q_norm_g': 1.0 + nrm(k[11], (hd,), 0.02),
        'k_cmp_norm_g': 1.0 + nrm(k[12], (hd,), 0.02),
        'k_slc_norm_g': 1.0 + nrm(k[13], (hd,), 0.02),
        'k_win_norm_g': 1.0 + nrm(k[14], (hd,), 0.02),
        'cmp_pe_k': nrm(k[15], (CMP_LEN, hd), 0.1),
        'cmp_w1_k': nrm(k[16], (CMP_LEN * hd, CMP_HIDDEN), (CMP_LEN * hd) ** -0.5),
        'cmp_w2_k': nrm(k[17], (CMP_HIDDEN, hd), CMP_HIDDEN ** -0.5),
        'cmp_pe_v': nrm(k[18], (CMP_LEN, hd), 0.1),
        'cmp_w1_v': nrm(k[19], (CMP_LEN * hd, CMP_HIDDEN), (CMP_LEN * hd) ** -0.5),
        'cmp_w2_v': nrm(k[20], (CMP_HIDDEN, hd), CMP_HIDDEN ** -0.5),
        'w_attn_out': nrm(k[21], (N_HEADS_2 * hd, d), (N_HEADS_2 * hd) ** -0.5),
        'w_out': nrm(k[22], (d, d), d ** -0.5),
        'norm2_g': 1.0 + nrm(k[23], (d,), 0.02),
        'w_up': nrm(k[24], (d, 2 * D_FF), d ** -0.5),
        'ffn_conv_w': nrm(k[25], (FFN_CONV_W, 2 * D_FF), FFN_CONV_W ** -0.5),
        'ffn_conv_b': nrm(k[26], (2 * D_FF,), 0.02),
        'w_down': nrm(k[27], (D_FF, d), D_FF ** -0.5),
    }

def second_block(x, norm1_g, w_in, rnn_conv_w, rnn_conv_b, rg_w_a, rg_b_a, rg_w_x, rg_b_x, lru_lambda,
              w_rnn_out, q_norm_g, k_cmp_norm_g, k_slc_norm_g, k_win_norm_g, cmp_pe_k, cmp_w1_k, cmp_w2_k,
              cmp_pe_v, cmp_w1_v, cmp_w2_v, w_attn_out, w_out, norm2_g, w_up, ffn_conv_w, ffn_conv_b, w_down):
    kvw = N_KV * HEAD_DIM
    sizes = [D_RNN, D_RNN, N_HEADS_2 * HEAD_DIM] + [kvw] * 6 + [3 * N_HEADS_2, D_MODEL, D_MODEL]
    splits = np.cumsum(sizes)[:-1].tolist()
    for _ in range(DEPTH):
        h = rms_norm_2(x, norm1_g)
        proj = h @ w_in
        (rx, rgate, q, kc, vc, ks, vs, kw, vw, nsa_g, mg_rnn, mg_attn) = jnp.split(proj, splits, axis=-1)
        hr = rg_lru(causal_dwconv(rx, rnn_conv_w, rnn_conv_b), rg_w_a, rg_b_a, rg_w_x, rg_b_x, lru_lambda)
        y_rnn = (hr * jax.nn.gelu(rgate)) @ w_rnn_out
        o = nsa(q, kc, vc, ks, vs, kw, vw, nsa_g, q_norm_g, k_cmp_norm_g, k_slc_norm_g, k_win_norm_g,
                cmp_pe_k, cmp_w1_k, cmp_w2_k, cmp_pe_v, cmp_w1_v, cmp_w2_v)
        y_attn = o @ w_attn_out
        x = x + (jax.nn.sigmoid(mg_rnn) * y_rnn + jax.nn.sigmoid(mg_attn) * y_attn) @ w_out
        up = causal_dwconv(rms_norm_2(x, norm2_g) @ w_up, ffn_conv_w, ffn_conv_b)
        gate, val = jnp.split(up, 2, axis=-1)
        x = x + (jax.nn.gelu(gate) * val) @ w_down
    return x


def setup_inputs(seed=0):
    out = dict(first_inputs(seed))
    for name, value in second_inputs(seed + 1).items():
        if name != "x":
            out[name + "_2"] = value
    return out


def reference(
    x, c, w_ada, b_ada, g_norm1, w_in, g_q, g_k, g_ik, w_pool_grp, s_pool, w_up_attn, w_up_pool,
    w_out, g_norm2, w_peer_q, peer_subkeys, peer_u, peer_v, norm1_g_2, w_in_2, rnn_conv_w_2,
    rnn_conv_b_2, rg_w_a_2, rg_b_a_2, rg_w_x_2, rg_b_x_2, lru_lambda_2, w_rnn_out_2, q_norm_g_2,
    k_cmp_norm_g_2, k_slc_norm_g_2, k_win_norm_g_2, cmp_pe_k_2, cmp_w1_k_2, cmp_w2_k_2,
    cmp_pe_v_2, cmp_w1_v_2, cmp_w2_v_2, w_attn_out_2, w_out_2, norm2_g_2, w_up_2, ffn_conv_w_2,
    ffn_conv_b_2, w_down_2,
):
    x = first_block(
        x, c, w_ada, b_ada, g_norm1, w_in, g_q, g_k, g_ik, w_pool_grp, s_pool, w_up_attn,
        w_up_pool, w_out, g_norm2, w_peer_q, peer_subkeys, peer_u, peer_v,
    )
    return second_block(
        x, norm1_g_2, w_in_2, rnn_conv_w_2, rnn_conv_b_2, rg_w_a_2, rg_b_a_2, rg_w_x_2,
        rg_b_x_2, lru_lambda_2, w_rnn_out_2, q_norm_g_2, k_cmp_norm_g_2, k_slc_norm_g_2,
        k_win_norm_g_2, cmp_pe_k_2, cmp_w1_k_2, cmp_w2_k_2, cmp_pe_v_2, cmp_w1_v_2, cmp_w2_v_2,
        w_attn_out_2, w_out_2, norm2_g_2, w_up_2, ffn_conv_w_2, ffn_conv_b_2, w_down_2,
    )


_drawn_inputs = setup_inputs


def setup_inputs(seed=0):
    import zlib

    import numpy as np

    out = dict(_drawn_inputs(seed))
    spreads = {}
    factors = {'g_norm1': 2.867,
     'g_q': 8.0,
     'g_k': 8.0,
     'g_ik': 4.374,
     'norm1_g_2': 6.183,
     'rg_b_a_2': 25.105,
     'rg_b_x_2': 8.0,
     'q_norm_g_2': 8.0,
     'k_cmp_norm_g_2': 46.894,
     'k_slc_norm_g_2': 8.0,
     'k_win_norm_g_2': 8.0,
     'cmp_pe_k_2': 8.0,
     'cmp_pe_v_2': 22.74,
     'norm2_g_2': 13.347,
     'ffn_conv_b_2': 13.43,
     'rnn_conv_b_2': 3.92}
    for name, (base, spread) in spreads.items():
        noise = np.random.default_rng([zlib.crc32(name.encode()), seed]).standard_normal(out[name].shape)
        drawn = base * np.exp(spread * noise) if base else spread * noise
        out[name] = jnp.asarray(drawn.astype(out[name].dtype))
    for name, factor in factors.items():
        out[name] = (out[name] * factor).astype(out[name].dtype)
    return out
```

```python
from contextlib import ExitStack

import numpy as np

import concourse.bass as bass
from concourse import mybir
from concourse.alu_op_type import AluOpType as ALU

ACT = mybir.ActivationFunctionType
F32 = mybir.dt.float32
U32 = mybir.dt.uint32
AX_X = mybir.AxisListType.X

P = 128
S = 256
T = S // P
D = 1024
KC = D // P
NB = 512
BLK = KC * NB
RING = 3
EPS = 1e-6
HD = 64
MASKED = -1e30
BARRED = -1e38
TAKEN = -3e38

H1, HI = 8, 4
Q1, K1, V1, IQ1 = 0, 512, 576, 640
IK1 = IQ1 + HI * HD
IW1 = IK1 + HD
P1 = IW1 + HI
G1 = P1 + 512
Z1W = 3524
Z1B = -(-Z1W // NB)
NSEL = 64
ADA_B = 6 * D // NB
PH, NK, TOPK = 8, 128, 16
SLOTS = PH * TOPK
I2_PER = 4
U_BLOCKS = NK // I2_PER
RB, RW = 16, 84
SUB = NB // RW
R_BLOCKS = -(-2 * RB // SUB)
H2, KV = 16, 4
KC2, VC2, KS2, VS2, KW2, VW2, MR2, MA2 = 1024, 1280, 1536, 1792, 2048, 2304, 2560, 3584
Z2W = 4608
Z2B = Z2W // NB
NCMP, CSTEP, CLEN = 15, 16, 32
FF = 3072
FT = FF // P
F_B = FF // NB

_COLS = [("cT", 8), ("g1", 8), ("g2", 8), ("bada", 48), ("gain1", 8), ("spool", 4), ("n1", 8), ("n2", 8),
         ("gainq", 1), ("gainks", 1), ("gainkw", 1), ("gainkc", 1), ("pek", 16), ("pev", 16),
         ("ffw", 3 * 2 * FT), ("ffb", 2 * FT), ("ba", RB), ("bx", RB), ("lam", RB), ("cw", 4 * RB), ("cb", RB)]
COL = {}
_at = 0
for _n, _w in _COLS:
    COL[_n] = (_at, _w)
    _at += _w
NCOL = _at


def plan():
    order = [f"ada{j}" for j in range(4)]
    for i in range(Z1B):
        order += [f"in{i}", f"ada{4 + i}"]
    order += ["ada11", "up_attn", "up_pool", "out0", "out1", "pq0", "pq1"]
    order += [f"u{m}" for m in range(U_BLOCKS)] + [f"v{m}" for m in range(U_BLOCKS)]
    order += [f"r{i}" for i in range(R_BLOCKS)] + ["z0", "z1", "rgate"] + [f"z{i}" for i in range(2, Z2B)]
    order += ["cmp"] + [f"ro{i}" for i in range(4)] + ["ao0", "ao1", "oo0", "oo1"]
    for f in range(F_B):
        order += [f"fg{f}", f"fv{f}"]
    return order + [f"dn{i}" for i in range(6)]


ORDER = plan()
AT = {n: i for i, n in enumerate(ORDER)}


def build_program(nc, a, out):
    ctx = ExitStack()
    with ctx:
        names = {}

        def sem(name):
            if name not in names:
                names[name] = ctx.enter_context(nc.semaphore(name))
            return names[name]

        def sb(name, shape, dt=F32):
            return ctx.enter_context(nc.sbuf_tensor(name, shape, dt))

        region = sb("region", [P, NK * S])
        ring = sb("ring", [P, RING, BLK])
        X = sb("X", [P, T, D])
        hT = sb("hT", [P, KC, S])
        ident = sb("ident", [P, P])
        iota = sb("iota", [P, P])
        ones = sb("ones", [P, P])
        cols = sb("cols", [P, NCOL])
        slotT = sb("slotT", [P, 3, S])
        adaT = sb("adaT", [P, 48])
        tiny = sb("tiny", [P, 64])
        PS = ctx.enter_context(nc.psum_tensor("PS", [P, 8, NB], F32))

        def col(name, i=0, n=P):
            o = COL[name][0] + i
            return cols[0:n, o:o + 1]

        def carve(start):
            at = [start]

            def take(*shape):
                n = int(np.prod(shape))
                v = region[:, at[0]:at[0] + n]
                at[0] += n
                assert at[0] <= NK * S, at[0]
                if len(shape) == 2:
                    v = v.rearrange("p (a b) -> p a b", a=shape[0])
                if len(shape) == 3:
                    v = v.rearrange("p (a b c) -> p a b c", a=shape[0], b=shape[1])
                if len(shape) == 4:
                    v = v.rearrange("p (a b c d) -> p a b c d", a=shape[0], b=shape[1], c=shape[2])
                return v
            return take

        take = carve(0)
        acc = take(2, NB)
        gate1 = take(D)
        XN1 = take(T, D)
        Z = take(T, Z1B * NB)
        N1 = take(T, D)
        NT1 = take(KC, S)
        band = take(T, 4, S)
        wpool = take(4, P)
        SK = take(PH, NK)
        brow = take(D)
        sq1 = take(T, 640)
        st1 = take(3, 2 * 10)
        score = take(T, S)
        work = take(T, S)
        stmp = take(S)
        m8 = take(8)
        bias1 = take(T, S)
        LB1 = take(3, S)
        PT1 = take(3, T, P)
        asm1 = take(4, 4)
        mixT = take(4, S)
        poolT = take(4, S)
        OT1 = take(4, S)
        M1, MT1 = N1, NT1
        mtmp = sq1.rearrange("p t n -> p (t n)")[:, 0:2 * NB].rearrange("p (t n) -> p t n", t=2)
        U_EARLY = 21
        take = carve(U_EARLY * I2_PER * S)
        SX = take(T, 2 * PH, NK)
        EQ = SX.rearrange("p t k n -> p (t k n)")[:, 0:PH * TOPK * TOPK].rearrange(
            "p (h k c) -> p h k c", h=PH, k=TOPK)
        TV = take(T, 2 * PH, TOPK)
        TI = take(T, 2 * PH, TOPK)
        CAND = take(PH, TOPK * TOPK)
        BV = take(T, PH, TOPK)
        BI = take(T, PH, TOPK)
        AB = take(2, PH, TOPK)
        BE = take(T, PH, TOPK)
        gsum = take(2, T * PH)
        SLOT = take(3, T, SLOTS)
        QTP = M1.rearrange("p t d -> p (t d)").rearrange("p (c s) -> p c s", c=KC)
        onehot = hT[:, :, :].rearrange("p c s -> p (c s)").rearrange("p (w g j k) -> p w g j k", w=2, g=2, j=4)
        take = carve(0)
        Z2 = take(T, Z2W)
        C2 = take(704)
        NSG = take(T, 48)
        XN2 = take(T, D)
        RX = take(RB, S)
        RGT = take(RB, S)
        XC = take(RB, S)
        RT = take(RB, S)
        IT = take(RB, S)
        sp = take(8, RB)
        M2 = XN2
        base = T * Z2W + 704 + T * 48 + T * D
        take = carve(base)
        N2 = take(T, D)
        QT2 = take(KC, S)
        KT2 = take(KC, S)
        CT2 = take(KC, S)
        take = carve(base + 3 * RB * S)
        SQ2 = take(T, 1536)
        st2 = take(3, 48)
        HID = take(2, P)
        kcmp = take(3, P)
        vcmp = take(HD)
        LC = take(T, S)
        cst = take(4, 32)
        PEB = take(2)
        LB2 = take(3, S)
        PT2 = take(3, T, P)
        asm2 = take(4, 4)
        f2 = take(2, NB)
        PZ = N2
        PZT = CT2
        OT2 = RX.rearrange("p b s -> p (b s)")[:, 0:0 + 2048].rearrange("p (c s) -> p c s", c=KC)
        MT2 = QT2
        take = carve(0)
        GV = take(FT, S)
        CG = take(4, S)
        CV = take(4, S)
        XN4 = XN2
        causal = C2[:, 0:512].rearrange("p (t s) -> p t s", t=T)
        cneg = C2[:, 512:544].rearrange("p (t s) -> p t s", t=T)
        c01 = C2[:, 544:576].rearrange("p (t s) -> p t s", t=T)
        w2k, w2v = C2[:, 576:640], C2[:, 640:704]

        loaded = [sem(f"block_loaded{i}") for i in range(RING)]
        used = [sem(f"block_used{i}") for i in range(RING)]

        def wait_loaded(eng, b):
            eng.wait_ge(loaded[b % RING], 16 * (b // RING + 1))

        def wait_used(eng, name):
            b = AT[name]
            eng.wait_ge(used[b % RING], b // RING + 1)

        def slot(name, inner=NB):
            return ring[:, AT[name] % RING, :].rearrange("p (c n) -> p c n", n=inner)

        def free_slot(name, ins):
            ins.then_inc(used[AT[name] % RING], 1)


        def units1():
            for t in range(T):
                for h in range(H1):
                    lo = HD * (h % 2)
                    yield dict(q=NT1[lo:lo + HD, h // 2, t * P:(t + 1) * P],
                               k=NT1[lo:lo + HD, 4, 0:(t + 1) * P], n=t + 1, mask=bias1[:, t, 0:(t + 1) * P],
                               v=[Z[:, j, V1:V1 + HD] for j in range(t + 1)], gate=None,
                               out=PS[lo:lo + HD, 4 + h // 4, (h // 2 % 2) * S + t * P:(h // 2 % 2) * S + (t + 1) * P],
                               start=True)

        def units2():
            for br, (ko, vo) in enumerate(((0, VS2), (4, VW2))):
                for t in range(T):
                    for h in range(H2):
                        lo, g, hp = HD * (h % 2), h // (H2 // KV), h // 2
                        yield dict(q=QT2[lo:lo + HD, hp, t * P:(t + 1) * P],
                                   k=KT2[lo:lo + HD, ko + g, 0:(t + 1) * P], n=t + 1,
                                   mask=causal[:, t, 0:(t + 1) * P],
                                   v=[Z2[:, j, vo + g * HD:vo + (g + 1) * HD] for j in range(t + 1)],
                                   gate=NSG[:, t, 3 * h + 1 + br:3 * h + 2 + br],
                                   out=PS[lo:lo + HD, 4 + hp // 2, (hp % 2) * S + t * P:(hp % 2) * S + (t + 1) * P],
                                   start=False)

        ATTN = {"a1": (list(units1()), LB1, PT1, asm1), "a2": (list(units2()), LB2, PT2, asm2)}

        block = ctx.enter_context(nc.Block())

        @block.sync
        def _(sp_):
            small = sem("small_loaded")
            sp_.dma_start(X[:, :, :], a["x"].rearrange("(t p) d -> p t d", p=P)).then_inc(small, 16)
            sp_.dma_start(cols[:, :], a["cols"]).then_inc(small, 16)
            sp_.dma_start(ident[:, :], a["consts"][:, 0:P]).then_inc(small, 16)
            sp_.dma_start(iota[:, :], a["consts"][:, P:2 * P]).then_inc(small, 16)
            sp_.dma_start(ones[:, :], a["consts"][:, 2 * P:3 * P]).then_inc(small, 16)
            for b in range(RING):
                sp_.dma_start(ring[:, b, :], a["stream"][b]).then_inc(loaded[b], 16)
            sp_.dma_start(brow[0:1, :], a["brow"]).then_inc(small, 16)
            sp_.dma_start(band, a["band"].rearrange("p (t g s) -> p t g s", t=T, g=4)).then_inc(small, 16)
            sp_.dma_start(wpool, a["wpool"].rearrange("p (g d) -> p g d", g=4)).then_inc(small, 16)
            sp_.dma_start(SK, a["skeys"].rearrange("p (h k) -> p h k", h=PH)).then_inc(small, 16)
            n = len(ORDER) // RING
            with sp_.Fori(1, n) as r:
                for i in range(RING):
                    sp_.wait_ge(used[i], r)
                    sp_.dma_start(ring[:, i, :], a["stream"][bass.ds(r * RING + i, 1)].rearrange(
                        "a p n -> p (a n)")).then_inc(loaded[i], 16)
            for b in range(n * RING, len(ORDER)):
                sp_.wait_ge(used[b % RING], b // RING)
                sp_.dma_start(ring[:, b % RING, :], a["stream"][b]).then_inc(loaded[b % RING], 16)
            sp_.wait_ge(sem("result_ready"), 4)
            sp_.dma_start(out.rearrange("(t p) d -> p t d", p=P), X[:, :, :]).then_inc(sem("stored"), 16)
            sp_.wait_ge(sem("stored"), 16)

        SMALL_ALL = 16 * 9

        @block.tensor
        def _(pe):
            def transposes(tag, src, ready, n_ready):
                pe.wait_ge(sem(ready), n_ready)
                for c in range(KC):
                    for t in range(T):
                        last = pe.transpose(PS[:, c // 2, (c % 2) * S + t * P:(c % 2) * S + (t + 1) * P],
                                            src[:, t, c * P:(c + 1) * P], ident[:, :])
                    if c % 2:
                        last.then_inc(sem(f"{tag}_turned"), 1)

            def ada(j):
                wait_used(pe, f"ada{j}")
                if j in (4, 5):
                    pe.matmul(PS[:, 1 + j, :], ones[:, :], acc[:, j % 2, :], start=True, stop=False)
                    last = pe.matmul(PS[:, 1 + j, :], ones[0:1, :], brow[0:1, (j - 4) * NB:(j - 3) * NB],
                                     start=False, stop=True)
                else:
                    for q in range(4):
                        last = pe.matmul(PS[:, 7, 4 * j + q:4 * j + q + 1], acc[:, j % 2, q * P:(q + 1) * P],
                                         ones[:, 0:1], start=True, stop=True)
                last.then_inc(sem("ada_summed"), 1)

            def project(name, t, bank, xT, w, chunks, rows=P, start=True, stop=True):
                for i, c in enumerate(chunks):
                    last = pe.matmul(PS[:, bank, 0:w.shape[-1]], xT[0:rows, c, t * P:(t + 1) * P], w[0:rows, i, :],
                                     start=start and i == 0, stop=stop and i == len(chunks) - 1)
                return last

            def attention(tag):
                units, LB, PT, asm = ATTN[tag]
                n = len(units)

                def logits(u):
                    x = units[u]
                    if u >= 2:
                        pe.wait_ge(sem(f"{tag}_max"), u - 1)
                    pe.matmul(PS[:, u % 2, 0:x["n"] * P], x["q"], x["k"], start=True,
                              stop=True).then_inc(sem(f"{tag}_logits"), 1)

                def turn(u):
                    x = units[u]
                    pe.wait_ge(sem(f"{tag}_norm"), u + 1)
                    if u >= 2:
                        pe.wait_ge(sem(f"{tag}_kept"), u - 1)
                    for j in range(x["n"]):
                        last = pe.transpose(PS[:, 2 + u % 2, j * P:(j + 1) * P], LB[:, u % 3, j * P:(j + 1) * P],
                                            ident[:, :])
                    last.then_inc(sem(f"{tag}_turned"), 1)

                def values(u):
                    x = units[u]
                    pe.wait_ge(sem(f"{tag}_kept"), u + 1)
                    for j in range(x["n"]):
                        last = pe.matmul(x["out"], x["v"][j], PT[:, u % 3, j, :], start=x["start"] and j == 0,
                                         stop=x["start"] and j == x["n"] - 1, skip_group_check=not x["start"])
                    last.then_inc(sem(f"{tag}_values"), 1)

                for u in range(n + 3):
                    if u < n:
                        logits(u)
                    if 0 <= u - 2 < n:
                        turn(u - 2)
                    if 0 <= u - 3 < n:
                        values(u - 3)

            pe.wait_ge(sem("small_loaded"), SMALL_ALL)
            for j in range(4):
                ada(j)
            transposes("n1", XN1, "n1_scaled", T)
            for i in range(Z1B):
                b = AT[f"in{i}"]
                wait_loaded(pe, b)
                if i == 0:
                    pe.wait_ge(sem("n1_kept"), KC)
                if i >= 2:
                    pe.wait_ge(sem("z_kept"), 2 * (i - 1))
                for t in range(T):
                    last = project("in", t, (2 * i + t) % 4, hT, slot(f"in{i}"), range(KC))
                free_slot(f"in{i}", last)
                ada(4 + i)
            ada(11)
            pe.wait_ge(sem("z_kept"), 2 * Z1B)
            for g in range(4):
                for t in range(T):
                    last = pe.matmul(PS[:, 2 + g // 2, (g % 2) * S:(g % 2 + 1) * S],
                                     Z[:, t, P1 + g * P:P1 + (g + 1) * P], band[:, t, g, :],
                                     start=(t == 0), stop=(t == T - 1))
            last.then_inc(sem("pool_meaned"), 1)
            pe.wait_ge(sem("gate1_kept"), 2)
            pe.wait_ge(sem("pool_means_kept"), 1)
            for g in range(4):
                last = pe.matmul(PS[:, 4 + g // 2, (g % 2) * S:(g % 2 + 1) * S], wpool[:, g, :], mixT[:, g, :],
                                 start=True, stop=True)
            last.then_inc(sem("pool_mixed"), 1)
            transposes("qk1", N1, "qk1_normed", 1)
            pe.wait_ge(sem("qk1_kept"), KC)
            pe.wait_ge(sem("pool_kept"), 4)
            pe.wait_ge(sem("ada_kept"), 2)
            for t in range(T):
                for h in range(HI):
                    lo = HD * (h % 2)
                    last = pe.matmul(PS[:, 4 + 2 * t + h % 2, (h // 2) * S:(h // 2) * S + (t + 1) * P],
                                     NT1[lo:lo + HD, 5 + h // 2, t * P:(t + 1) * P],
                                     NT1[lo:lo + HD, 7, 0:(t + 1) * P], start=True, stop=True)
                last.then_inc(sem("index_products"), 1)
            pe.wait_ge(sem("chosen"), T)
            attention("a1")
            pe.wait_ge(sem("attn1_kept"), 4)
            for name, src, b0 in (("up_attn", OT1, 0), ("up_pool", poolT, 4)):
                wait_loaded(pe, AT[name])
                w = slot(name, D)
                for t in range(T):
                    for half in range(2):
                        last = project(name, t, b0 + 2 * t + half, src, w[:, :, half * NB:(half + 1) * NB], range(4))
                free_slot(name, last)
            transposes("m1", M1, "m1_ready", 1)
            pe.wait_ge(sem("m1_kept"), KC)
            for half in range(2):
                wait_loaded(pe, AT[f"out{half}"])
                for t in range(T):
                    last = project("out", t, 4 + 2 * t + half, MT1, slot(f"out{half}"), range(KC))
                free_slot(f"out{half}", last)
            transposes("n2", XN1, "n2_scaled", T)
            pe.wait_ge(sem("n2_kept"), KC)
            for i in range(2):
                wait_loaded(pe, AT[f"pq{i}"])
                w = slot(f"pq{i}")
                for hh in range(4):
                    h = 4 * i + hh
                    for c in range(KC):
                        last = pe.matmul(PS[:, h // 2, (h % 2) * S:(h % 2 + 1) * S], w[:, c, hh * P:(hh + 1) * P],
                                         hT[:, c, :], start=(c == 0), stop=(c == KC - 1))
                free_slot(f"pq{i}", last)
            pe.wait_ge(sem("peer_q_kept"), 4)
            for t in range(T):
                for h in range(PH):
                    for p in range(2):
                        last = pe.matmul(PS[:, 4 * t + 2 * (h // 4) + p, (h % 4) * NK:(h % 4 + 1) * NK],
                                         QTP[HD * p:HD * (p + 1), h, t * P:(t + 1) * P],
                                         SK[HD * p:HD * (p + 1), h, :], start=True, stop=True)
                    if h % 4 == 3:
                        last.then_inc(sem("peer_scored"), 1)

            def peer_u(m, r=0):
                b = AT["u0"] + m
                pe.wait_ge(loaded[b % RING], 16 * (b // RING + 1) + 16 * r)
                pe.wait_ge(sem("u_banks_free"), 2 * m + 2 + 6 * r)
                w = ring[:, b % RING, :].rearrange("p (i c k) -> p i c k", i=I2_PER, c=KC)
                for i in range(I2_PER):
                    for c in range(KC):
                        last = pe.matmul(PS[:, 2 * (m % 3) + i // 2, (i % 2) * S:(i % 2 + 1) * S], w[:, i, c, :],
                                         hT[:, c, :], start=(c == 0), stop=(c == KC - 1))
                last.then_inc(used[b % RING], 1)

            with pe.Fori(0, U_EARLY // 3) as r:
                for k in range(3):
                    peer_u(k, r)
            pe.wait_ge(sem("slots_ready"), 1)
            for w in range(3):
                for t in range(T):
                    last = pe.transpose(PS[:, 6 + w // 2, (w % 2) * S + t * P:(w % 2) * S + (t + 1) * P],
                                        SLOT[:, w, t, :], ident[:, :])
            last.then_inc(sem("slots_turned"), 1)
            with pe.Fori(U_EARLY // 3, U_BLOCKS // 3) as r:
                for k in range(3):
                    peer_u(k, r)
            for m in range(U_BLOCKS // 3 * 3, U_BLOCKS):
                peer_u(m)

            def gates(g, r=0):
                pe.wait_ge(sem("onehot_ready"), g + 1 + 2 * r)
                pe.wait_ge(sem("gate_banks_free"), g + 1 + 2 * r)
                for j in range(4):
                    last = pe.matmul(PS[:, g % 2, j * P:(j + 1) * P], onehot[:, 0, g % 2, j, :],
                                     onehot[:, 1, g % 2, j, :], start=True, stop=True)
                last.then_inc(sem("gates_placed"), 1)

            pe.sem_inc(sem("gates_placed"), 1)
            with pe.Fori(0, S // 8) as r:
                for g in range(2):
                    gates(g, r)

            def peer_v(m, r=0):
                b = AT["v0"] + m
                pe.wait_ge(loaded[b % RING], 16 * (b // RING + 1) + 16 * r)
                w = ring[:, b % RING, :].rearrange("p (i d) -> p i d", i=I2_PER)
                for i in range(I2_PER):
                    for c in range(KC):
                        last = pe.matmul(PS[:, 4 + c // 2, (c % 2) * S:(c % 2 + 1) * S], w[:, i, c * P:(c + 1) * P],
                                         region[:, bass.ds((m * I2_PER + i) * S + r * (3 * I2_PER * S), S)],
                                         start=(isinstance(r, int) and m == 0 and i == 0 and c % 2 == 0),
                                         stop=(m == U_BLOCKS - 1 and i == I2_PER - 1), skip_group_check=True)
                last.then_inc(used[b % RING], 1)

            pe.wait_ge(sem("weighted"), 1)
            peer_v(0)
            with pe.Fori(0, (U_BLOCKS - 1) // 3) as r:
                for k in range(1, 4):
                    peer_v(k, r)
            for m in range((U_BLOCKS - 1) // 3 * 3 + 1, U_BLOCKS):
                peer_v(m)
            pe.wait_ge(sem("peer_out_kept"), KC)
            for t in range(T):
                for half in range(2):
                    for c in range(4):
                        last = pe.transpose(PS[:, 2 * t + half, c * P:(c + 1) * P],
                                            hT[:, 4 * half + c, t * P:(t + 1) * P], ident[:, :])
                    last.then_inc(sem("peer_out_turned"), 1)

            transposes("n3", XN2, "n3_scaled", T)
            pe.wait_ge(sem("n3_kept"), KC)
            for i in range(R_BLOCKS):
                wait_loaded(pe, AT[f"r{i}"])
                if i >= 2:
                    pe.wait_ge(sem("r_kept"), SUB * (i - 1))
                w = slot(f"r{i}")
                subs = range(SUB * i, min(SUB * (i + 1), 2 * RB))
                for k, s in enumerate(subs):
                    for c in range(KC):
                        last = pe.matmul(PS[0:RW, 3 * (i % 2) + k // 2, (k % 2) * S:(k % 2 + 1) * S],
                                         w[:, c, k * RW:(k + 1) * RW], hT[:, c, :], start=(c == 0), stop=(c == KC - 1))
                if i == R_BLOCKS - 1:
                    o = len(subs) * RW
                    for t in range(T):
                        for c in range(KC):
                            last = pe.matmul(PS[:, 4, t * HD:t * HD + 48], hT[:, c, t * P:(t + 1) * P],
                                             w[:, c, o:o + 48], start=(c == 0), stop=(c == KC - 1))
                free_slot(f"r{i}", last)

            def z2(i):
                wait_loaded(pe, AT[f"z{i}"])
                if i < 2:
                    pe.wait_ge(sem("r_kept"), 2 * RB + T)
                else:
                    pe.wait_ge(sem("z2_kept"), 2 * (i - 1))
                for t in range(T):
                    last = project("z", t, 4 + (2 * i + t) % 4, hT, slot(f"z{i}"), range(KC))
                free_slot(f"z{i}", last)

            z2(0)
            z2(1)
            wait_loaded(pe, AT["rgate"])
            w = ring[0:RW, AT["rgate"] % RING, 0:2 * RB * RW].rearrange("p (w b n) -> p w b n", w=2, b=RB)
            for n in range(RB):
                pe.wait_ge(sem("conv_done"), n + 1)
                if n >= 4:
                    pe.wait_ge(sem("rgate_kept"), 2 * (n - 3))
                for k in range(2):
                    last = pe.matmul(PS[0:RW, n % 4, k * S:(k + 1) * S], w[:, k, n, :], XC[0:RW, n, :],
                                     start=True, stop=True)
                if n < RB - 1:
                    last.then_inc(sem("rgate_done"), 1)
            free_slot("rgate", last)
            for i in range(2, Z2B):
                z2(i)
            pe.wait_ge(sem("z2_kept"), 2 * Z2B)
            pe.wait_ge(sem("rec_out"), 1)
            transposes("q2", N2, "q2_normed", 1)
            pe.wait_ge(sem("q2_kept"), KC)
            transposes("k2", N2, "k2_normed", 1)
            pe.wait_ge(sem("k2_kept"), KC)
            transposes("c2", N2, "c2_copied", 1)
            pe.wait_ge(sem("c2_kept"), 2 * KC)
            wait_loaded(pe, AT["cmp"])
            w = ring[:, AT["cmp"] % RING, :].rearrange("p (w l n) -> p w l n", w=2, l=CLEN // 2)
            for kv in range(2):
                for l in range(CLEN // 2):
                    pe.matmul(PS[:, kv, 0:KV * NCMP], w[:, kv, l, :],
                              CT2[:, KV * kv:KV * (kv + 1), 2 * l:2 * l + CSTEP * (NCMP - 1) + 1:CSTEP],
                              start=(l == 0), stop=(l == CLEN // 2 - 1))
                for l in range(CLEN // 2):
                    last = pe.matmul(PS[:, 2 + kv, 0:1], w[:, kv, l, :], col("pek" if kv == 0 else "pev", l),
                                     start=(l == 0), stop=(l == CLEN // 2 - 1))
            free_slot("cmp", last)
            for i in range(4):
                wait_loaded(pe, AT[f"ro{i}"])
                w = slot(f"ro{i}", D)
                for t in range(T):
                    for half in range(2):
                        last = project("ro", t, 4 + 2 * t + half, XC, w[:, :, half * NB:(half + 1) * NB],
                                       range(4 * i, 4 * i + 4), rows=RW, start=(i == 0), stop=(i == 3))
                free_slot(f"ro{i}", last)
            pe.wait_ge(sem("hidden_kept"), 3)
            pe.wait_ge(sem("consts2_loaded"), 16)
            pe.matmul(PS[0:HD, 0, 128:128 + HD], HID[:, 0, 0:HD], w2k, start=True, stop=True)
            pe.matmul(PS[:, 1, 128:128 + HD], HID[:, 1, :], w2v, start=True, stop=True).then_inc(sem("cmp_made"), 1)
            pe.wait_ge(sem("kcmp_normed"), 1)
            pe.transpose(PS[:, 2, 0:HD], kcmp[0:HD, 1, :], ident[0:HD, 0:HD]).then_inc(sem("kcmp_turned"), 1)
            pe.wait_ge(sem("kcmp_kept"), 1)
            for t in range(T):
                for h in range(H2):
                    lo, g = HD * (h % 2), h // (H2 // KV)
                    o = (t * H2 // 2 + h // 2) * 16
                    last = pe.matmul(PS[:, 3 * (h % 2), o:o + 16],
                                     QT2[lo:lo + HD, h // 2, t * P:(t + 1) * P],
                                     kcmp[lo:lo + HD, 2, g * 16:(g + 1) * 16], start=True, stop=True)
            last.then_inc(sem("cmp_logits"), 1)
            pe.wait_ge(sem("rec_gated"), 4)
            transposes("pz", PZ, "cmp_probs", 1)
            pe.wait_ge(sem("pz_kept"), KC)
            for h in range(H2):
                lo, hp = HD * (h % 2), h // 2
                pe.matmul(PS[lo:lo + HD, 4 + hp // 2, (hp % 2) * S:(hp % 2 + 1) * S], vcmp[lo:lo + HD, :],
                          PZT[lo:lo + HD, hp, :], start=(hp % 2 == 0), stop=False, skip_group_check=True)
            attention("a2")
            pe.wait_ge(sem("attn2_kept"), KC)
            for half in range(2):
                wait_loaded(pe, AT[f"ao{half}"])
                for t in range(T):
                    last = project("ao", t, 2 * t + half, OT2, slot(f"ao{half}"), range(KC))
                free_slot(f"ao{half}", last)
            transposes("m2", M2, "m2_ready", 4)
            pe.wait_ge(sem("m2_kept"), KC)
            for half in range(2):
                wait_loaded(pe, AT[f"oo{half}"])
                for t in range(T):
                    last = project("oo", t, 4 + 2 * t + half, MT2, slot(f"oo{half}"), range(KC))
                free_slot(f"oo{half}", last)
            transposes("n4", XN4, "n4_scaled", T)
            pe.wait_ge(sem("n4_kept"), KC)
            for f in range(F_B):
                for w_, name in enumerate(("fg", "fv")):
                    wait_loaded(pe, AT[f"{name}{f}"])
                    if f >= 2:
                        pe.wait_ge(sem(f"{name}_read"), 4 * (f - 1))
                    w = slot(f"{name}{f}")
                    for q in range(4):
                        for c in range(KC):
                            last = pe.matmul(PS[:, 4 * (f % 2) + 2 * w_ + q // 2, (q % 2) * S:(q % 2 + 1) * S],
                                             w[:, c, q * P:(q + 1) * P], hT[:, c, :], start=(c == 0),
                                             stop=(c == KC - 1))
                    free_slot(f"{name}{f}", last)
            for i in range(6):
                wait_loaded(pe, AT[f"dn{i}"])
                pe.wait_ge(sem("ffn_gated"), 4 * (i + 1))
                if i == 0:
                    pe.wait_ge(sem("fv_read"), 4 * (F_B - 1))
                w = slot(f"dn{i}", D)
                for t in range(T):
                    for half in range(2):
                        last = project("dn", t, 2 * t + half, GV, w[:, :, half * NB:(half + 1) * NB],
                                       range(4 * i, 4 * i + 4), start=(i == 0), stop=(i == 5))
                free_slot(f"dn{i}", last)

        @block.scalar
        def _(act):
            steps = [0]

            def link(ins):
                steps[0] += 1
                ins.then_inc(sem("act_step"), 1)
                act.wait_ge(sem("act_step"), steps[0])

            def sumsq(tag, XN, ready=None, n=0):
                if ready:
                    act.wait_ge(sem(ready), n)
                for t in range(T):
                    act.activation(XN[:, t, :], X[:, t, :], ACT.Square,
                                   accum_out=tiny[:, t:t + 1]).then_inc(sem(f"{tag}_sumsq"), 1)
                act.wait_ge(sem(f"{tag}_meansq"), 1)
                act.activation(tiny[:, 4:4 + T], tiny[:, 2:2 + T], ACT.Sqrt).then_inc(sem(f"{tag}_root"), 1)

            def keep_turned(tag, dst, scale=None, shift=None):
                for c in range(KC // 2):
                    act.wait_ge(sem(f"{tag}_turned"), c // 2 + 1)
                    kw = {}
                    if scale:
                        kw["scale"] = scale(c)
                    if shift:
                        kw["bias"] = shift(c)
                    act.activation(dst[:, c, :], PS[:, c // 2, (c % 2) * S:(c % 2 + 1) * S],
                                   ACT.Identity if kw else ACT.Copy, **kw).then_inc(sem(f"{tag}_kept"), 1)

            def attention(tag, scale):
                units, LB, PT, asm = ATTN[tag]
                n = len(units)

                def kept(u):
                    x = units[u]
                    act.wait_ge(sem(f"{tag}_turned"), u + 1)
                    if u >= 3:
                        act.wait_ge(sem(f"{tag}_values"), u - 2)
                    act.activation(PT[:, u % 3, 0:x["n"], :].rearrange("p j q -> p (j q)"),
                                   PS[:, 2 + u % 2, 0:x["n"] * P], ACT.Copy).then_inc(sem(f"{tag}_kept"), 1)

                for u in range(n + 2):
                    if u < n:
                        x = units[u]
                        act.wait_ge(sem(f"{tag}_negmax"), u + 1)
                        act.activation(LB[:, u % 3, 0:x["n"] * P], LB[:, u % 3, 0:x["n"] * P], ACT.Exp, scale=scale,
                                       bias=asm[:, 1, u % 3:u % 3 + 1],
                                       accum_out=asm[:, 2, u % 3:u % 3 + 1]).then_inc(sem(f"{tag}_exp"), 1)
                    if 0 <= u - 2 < n:
                        kept(u - 2)

            act.wait_ge(sem("small_loaded"), SMALL_ALL)
            sumsq("n1", XN1)
            act.wait_ge(sem("mod1"), 1)
            keep_turned("n1", hT, lambda c: adaT[:, 8 + c:9 + c], lambda c: adaT[:, c:c + 1])
            for i in range(Z1B):
                wait_used(act, f"in{i}")
                for t in range(T):
                    act.activation(Z[:, t, i * NB:(i + 1) * NB], PS[:, (2 * i + t) % 4, :],
                                   ACT.Copy).then_inc(sem("z_kept"), 1)
                if i in (1, 2):
                    act.wait_ge(sem("ada_summed"), 4 + i)
                    act.activation(gate1[:, (i - 1) * NB:i * NB], PS[:, 4 + i, :],
                                   ACT.Copy).then_inc(sem("gate1_kept"), 1)
            act.wait_ge(sem("qk1_meansq"), 1)
            act.activation(st1[:, 1, :], st1[:, 0, :], ACT.Sqrt).then_inc(sem("qk1_root"), 1)
            act.wait_ge(sem("pool_meaned"), 1)
            act.activation(mixT.rearrange("p g s -> p (g s)"), PS[:, 2:4, :].rearrange("p b n -> p (b n)"),
                           ACT.Copy).then_inc(sem("pool_means_kept"), 1)
            act.wait_ge(sem("pool_mixed"), 1)
            for g in range(4):
                act.activation(poolT[:, g, :], PS[:, 4 + g // 2, (g % 2) * S:(g % 2 + 1) * S], ACT.Copy,
                               scale=col("spool", g)).then_inc(sem("pool_kept"), 1)
            keep_turned("qk1", NT1, lambda c: col("gain1", c))
            act.wait_ge(sem("z_kept"), 2 * Z1B)
            for t in range(T):
                act.activation(Z[:, t, G1:G1 + 2 * D], Z[:, t, G1:G1 + 2 * D],
                               ACT.Sigmoid).then_inc(sem("sig1"), 1)
            attention("a1", HD ** -0.5)
            act.wait_ge(sem("a1_values"), len(ATTN["a1"][0]))
            for c in range(4):
                act.activation(OT1[:, c, :], PS[:, 4 + c // 2, (c % 2) * S:(c % 2 + 1) * S],
                               ACT.Copy).then_inc(sem("attn1_kept"), 1)
            keep_turned("m1", MT1)
            sumsq("n2", XN1, "x1_ready", 4)
            keep_turned("n2", hT, lambda c: adaT[:, 32 + c:33 + c], lambda c: adaT[:, 24 + c:25 + c])
            for i in range(2):
                wait_used(act, f"pq{i}")
                for j in range(2):
                    act.activation(QTP[:, 4 * i + 2 * j:4 * i + 2 * j + 2, :].rearrange("p c s -> p (c s)"),
                                   PS[:, 2 * i + j, :], ACT.Copy).then_inc(sem("peer_q_kept"), 1)
            for i in range(8):
                t, q, p = i // 4, i // 2 % 2, i % 2
                act.wait_ge(sem("peer_scored"), i // 2 + 1)
                act.activation(SX[:, t, :, :].rearrange("p (h w) n -> p w h n", w=2)[:, p, 4 * q:4 * q + 4, :],
                               PS[:, i, :].rearrange("p (h n) -> p h n", h=4),
                               ACT.Copy).then_inc(sem("scores_kept"), 1)
            act.wait_ge(sem("scores_kept"), 8)
            act.sem_inc(sem("u_banks_free"), 6)

            def gelu_u(m, r=0):
                b = AT["u0"] + m
                act.wait_ge(used[b % RING], b // RING + 1 + r)
                for j in range(2):
                    act.activation(region[:, bass.ds((m * I2_PER + 2 * j) * S + r * (3 * I2_PER * S), 2 * S)],
                                   PS[:, 2 * (m % 3) + j, :], ACT.Gelu).then_inc(sem("u_banks_free"), 1)

            with act.Fori(0, U_EARLY // 3) as r:
                for k in range(3):
                    gelu_u(k, r)
            act.wait_ge(sem("best_less_max"), 1)
            act.activation(BE.rearrange("p t h k -> p (t h k)"), BE.rearrange("p t h k -> p (t h k)"),
                           ACT.Exp).then_inc(sem("best_exp"), 1)
            act.wait_ge(sem("slots_saved"), 3)
            with act.Fori(U_EARLY // 3, U_BLOCKS // 3) as r:
                for k in range(3):
                    gelu_u(k, r)
            for m in range(U_BLOCKS // 3 * 3, U_BLOCKS):
                gelu_u(m)
            act.wait_ge(used[(AT["v0"] + U_BLOCKS - 1) % RING], (AT["v0"] + U_BLOCKS - 1) // RING + 1)
            act.dma_start(C2, a["consts2"]).then_inc(sem("consts2_loaded"), 16)
            for c in range(KC // 2):
                act.activation(hT[:, c, :], PS[:, 4 + c // 2, (c % 2) * S:(c % 2 + 1) * S], ACT.Copy,
                               scale=adaT[:, 40 + c:41 + c]).then_inc(sem("peer_out_kept"), 1)

            sumsq("n3", XN2, "x2_ready", 4)
            keep_turned("n3", hT, lambda c: col("n1", c))
            act.wait_ge(sem("lam_abs"), 1)
            act.activation(sp[0:RW, 1, :], sp[0:RW, 0, :], ACT.Exp, scale=-1.0).then_inc(sem("lam_exp"), 1)
            for i in range(R_BLOCKS):
                wait_used(act, f"r{i}")
                for k, s in enumerate(range(SUB * i, min(SUB * (i + 1), 2 * RB))):
                    dst = RX[0:RW, s, :] if s < RB else RGT[0:RW, s - RB, :]
                    act.activation(dst, PS[0:RW, 3 * (i % 2) + k // 2, (k % 2) * S:(k % 2 + 1) * S],
                                   ACT.Copy if s < RB else ACT.Gelu_apprx_tanh).then_inc(sem("r_kept"), 1)
            for t in range(T):
                act.activation(NSG[:, t, :], PS[:, 4, t * HD:t * HD + 48], ACT.Sigmoid).then_inc(sem("r_kept"), 1)

            def z2(i):
                wait_used(act, f"z{i}")
                for t in range(T):
                    act.activation(Z2[:, t, i * NB:(i + 1) * NB], PS[:, 4 + (2 * i + t) % 4, :],
                                   ACT.Copy).then_inc(sem("z2_kept"), 1)

            z2(0)
            z2(1)
            act.wait_ge(sem("decay_ready"), 1)
            for n in range(RB):
                if n < RB - 1:
                    act.wait_ge(sem("rgate_done"), n + 1)
                else:
                    wait_used(act, "rgate")
                act.activation(RT[0:RW, n, :], PS[0:RW, n % 4, 0:S], ACT.Sigmoid,
                               bias=col("ba", n, RW)).then_inc(sem("rgate_kept"), 1)
                act.activation(IT[0:RW, n, :], PS[0:RW, n % 4, S:2 * S], ACT.Sigmoid,
                               bias=col("bx", n, RW)).then_inc(sem("rgate_kept"), 1)
            for n in range(RB):
                act.wait_ge(sem("rgate_kept"), 2 * n + 2)
                act.activation(RT[0:RW, n, :], RT[0:RW, n, :], ACT.Tanh,
                               scale=sp[0:RW, 7, n:n + 1]).then_inc(sem("tanh_done"), 1)
            act.wait_ge(sem("tanh_done"), RB)
            act.wait_ge(sem("xc_used"), 1)
            act.activation(XC[0:RW, :, :].rearrange("p b s -> p (b s)"),
                           RT[0:RW, :, :].rearrange("p b s -> p (b s)"), ACT.Sqrt).then_inc(sem("root_tanh"), 1)
            for i in range(2, Z2B):
                z2(i)
            act.wait_ge(sem("z2_kept"), 2 * Z2B)
            act.wait_ge(sem("rec_out"), 1)
            for t in range(T):
                act.activation(SQ2[:, t, 0:1024], Z2[:, t, 0:1024], ACT.Square).then_inc(sem("sq2"), 1)
                act.activation(SQ2[:, t, 1024:1280], Z2[:, t, KS2:KS2 + 256], ACT.Square).then_inc(sem("sq2"), 1)
                act.activation(SQ2[:, t, 1280:1536], Z2[:, t, KW2:KW2 + 256], ACT.Square).then_inc(sem("sq2"), 1)
            act.wait_ge(sem("qk2_meansq"), 1)
            act.activation(st2[:, 1, :], st2[:, 0, :], ACT.Sqrt).then_inc(sem("qk2_root"), 1)
            keep_turned("q2", QT2, lambda c: col("gainq"))
            keep_turned("k2", KT2, lambda c: col("gainks"))
            for c in range(KC // 2):
                act.wait_ge(sem("c2_turned"), c // 2 + 1)
                src = PS[:, c // 2, (c % 2) * S:(c % 2 + 1) * S]
                act.activation(CT2[0:HD, c, :], src[0:HD, :], ACT.Copy).then_inc(sem("c2_kept"), 1)
                act.activation(CT2[HD:P, c, 0:S - 1], src[HD:P, 1:S], ACT.Copy).then_inc(sem("c2_kept"), 1)
            for t in range(T):
                act.activation(Z2[:, t, MR2:MR2 + 2 * D], Z2[:, t, MR2:MR2 + 2 * D],
                               ACT.Sigmoid).then_inc(sem("sig2"), 1)
            wait_used(act, "cmp")
            act.wait_ge(sem("pe_bias"), 1)
            hk = HID[:, 0, 0:HD].rearrange("p (g i) -> p g i", g=KV)[:, :, 0:NCMP]
            act.activation(hk, PS[:, 0, 0:KV * NCMP].rearrange("p (g i) -> p g i", g=KV), ACT.Gelu_apprx_tanh,
                           bias=PEB[:, 0:1]).then_inc(sem("hidden_kept"), 1)
            for dup in range(2):
                hv = HID[:, 1, dup * HD:(dup + 1) * HD].rearrange("p (g i) -> p g i", g=KV)[:, :, 0:NCMP]
                act.activation(hv, PS[:, 1, 0:KV * NCMP].rearrange("p (g i) -> p g i", g=KV), ACT.Gelu_apprx_tanh,
                               bias=PEB[:, 1:2]).then_inc(sem("hidden_kept"), 1)
            act.wait_ge(sem("kcmp_meansq"), 1)
            act.activation(cst[0:HD, 1, 0:1], cst[0:HD, 0, 0:1], ACT.Sqrt).then_inc(sem("kcmp_root"), 1)
            act.wait_ge(sem("cmp_less_max"), 1)
            act.activation(LC.rearrange("p t s -> p (t s)"), LC.rearrange("p t s -> p (t s)"),
                           ACT.Exp).then_inc(sem("cmp_exp"), 1)
            keep_turned("pz", PZT)
            attention("a2", HD ** -0.5)
            act.wait_ge(sem("a2_values"), len(ATTN["a2"][0]))
            for c in range(KC):
                act.activation(OT2[:, c, :], PS[:, 4 + c // 2, (c % 2) * S:(c % 2 + 1) * S],
                               ACT.Copy).then_inc(sem("attn2_kept"), 1)
            keep_turned("m2", MT2)
            sumsq("n4", XN4, "x3_ready", 4)
            keep_turned("n4", hT, lambda c: col("n2", c))
            for f in range(F_B):
                for q in range(4):
                    act.wait_ge(sem("fg_conv"), 4 * f + q + 1)
                    act.activation(CG[:, q, :], CG[:, q, :], ACT.Gelu_apprx_tanh).then_inc(sem("fg_gelu"), 1)

        @block.vector
        def _(dve):
            steps = [0]

            def link(ins):
                steps[0] += 1
                ins.then_inc(sem("dve_step"), 1)
                dve.wait_ge(sem("dve_step"), steps[0])

            def scaled(tag, XN):
                dve.wait_ge(sem(f"{tag}_sumsq"), T)
                dve.tensor_scalar(tiny[:, 2:2 + T], tiny[:, 0:T], 1.0 / D, EPS, ALU.mult,
                                  ALU.add).then_inc(sem(f"{tag}_meansq"), 1)
                dve.wait_ge(sem(f"{tag}_root"), 1)
                link(dve.reciprocal(tiny[:, 6:6 + T], tiny[:, 4:4 + T]))
                for t in range(T):
                    dve.tensor_scalar(XN[:, t, :], X[:, t, :], tiny[:, 6 + t:7 + t], None,
                                      ALU.mult).then_inc(sem(f"{tag}_scaled"), 1)

            def keep_turned(tag, dst, scale=None, shift=None):
                for c in range(KC // 2, KC):
                    dve.wait_ge(sem(f"{tag}_turned"), c // 2 + 1)
                    src = PS[:, c // 2, (c % 2) * S:(c % 2 + 1) * S]
                    if scale and shift:
                        ins = dve.tensor_scalar(dst[:, c, :], src, scale(c), shift(c), ALU.mult, ALU.add)
                    elif scale:
                        ins = dve.tensor_scalar(dst[:, c, :], src, scale(c), None, ALU.mult)
                    else:
                        ins = dve.tensor_copy(dst[:, c, :], src)
                    ins.then_inc(sem(f"{tag}_kept"), 1)

            def attention(tag, scale):
                units, LB, PT, asm = ATTN[tag]
                n = len(units)
                for u in range(n + 1):
                    if u < n:
                        x = units[u]
                        dve.wait_ge(sem(f"{tag}_logits"), u + 1)
                        if u >= 3:
                            dve.wait_ge(sem(f"{tag}_turned"), u - 2)
                        dve.tensor_tensor_reduce(LB[:, u % 3, 0:x["n"] * P], PS[:, u % 2, 0:x["n"] * P], x["mask"],
                                                 1.0, TAKEN, ALU.add, ALU.max,
                                                 asm[:, 0, u % 3:u % 3 + 1]).then_inc(sem(f"{tag}_max"), 1)
                        dve.wait_ge(sem(f"{tag}_max"), u + 1)
                        dve.tensor_scalar(asm[:, 1, u % 3:u % 3 + 1], asm[:, 0, u % 3:u % 3 + 1], -scale, None,
                                          ALU.mult).then_inc(sem(f"{tag}_negmax"), 1)
                    if u >= 1:
                        v, x = (u - 1) % 3, units[u - 1]
                        dve.wait_ge(sem(f"{tag}_exp"), u)
                        link(dve.reciprocal(asm[:, 3, v:v + 1], asm[:, 2, v:v + 1]))
                        if x["gate"] is None:
                            ins = dve.tensor_scalar(LB[:, v, 0:x["n"] * P], LB[:, v, 0:x["n"] * P],
                                                    asm[:, 3, v:v + 1], None, ALU.mult)
                        else:
                            ins = dve.tensor_scalar(LB[:, v, 0:x["n"] * P], LB[:, v, 0:x["n"] * P],
                                                    asm[:, 3, v:v + 1], x["gate"], ALU.mult, ALU.mult)
                        ins.then_inc(sem(f"{tag}_norm"), 1)

            def bc(ap, axis, n):
                v = ap.unsqueeze(axis)
                shape = list(v.shape)
                shape[axis] = n
                return v.broadcast_to(shape)

            def ada(j):
                wait_loaded(dve, AT[f"ada{j}"])
                if j >= 2:
                    dve.wait_ge(sem("ada_summed"), j - 1)
                w = slot(f"ada{j}")
                link(dve.tensor_scalar(acc[:, j % 2, :], w[:, 0, :], col("cT", 0), None, ALU.mult))
                for c in range(1, KC):
                    ins = dve.scalar_tensor_tensor(acc[:, j % 2, :], w[:, c, :], col("cT", c), acc[:, j % 2, :],
                                                   ALU.mult, ALU.add)
                    if c < KC - 1:
                        link(ins)
                free_slot(f"ada{j}", ins)

            dve.wait_ge(sem("small_loaded"), SMALL_ALL)
            scaled("n1", XN1)
            for j in range(4):
                ada(j)
            dve.wait_ge(sem("ada_summed"), 4)
            link(dve.tensor_tensor(adaT[:, 0:16], PS[:, 7, 0:16], cols[:, COL["bada"][0]:COL["bada"][0] + 16], ALU.add))
            dve.scalar_tensor_tensor(adaT[:, 8:16], adaT[:, 8:16], 1.0, cols[:, COL["g1"][0]:COL["g1"][0] + 8],
                                     ALU.add, ALU.mult).then_inc(sem("mod1"), 1)
            dve.wait_ge(sem("mod1"), 1)
            keep_turned("n1", hT, lambda c: adaT[:, 8 + c:9 + c], lambda c: adaT[:, c:c + 1])
            for j in range(4, ADA_B):
                ada(j)
            dve.wait_ge(sem("ada_summed"), ADA_B)
            dve.tensor_tensor(adaT[:, 24:48], PS[:, 7, 24:48],
                              cols[:, COL["bada"][0] + 24:COL["bada"][0] + 48], ALU.add).then_inc(sem("ada_kept"), 1)
            dve.wait_ge(sem("ada_kept"), 1)
            dve.scalar_tensor_tensor(adaT[:, 32:40], adaT[:, 32:40], 1.0, cols[:, COL["g2"][0]:COL["g2"][0] + 8],
                                     ALU.add, ALU.mult).then_inc(sem("ada_kept"), 1)
            dve.wait_ge(sem("z_kept"), 2 * Z1B)
            for t in range(T):
                link(dve.tensor_tensor(sq1[:, t, 0:576], Z[:, t, 0:576], Z[:, t, 0:576], ALU.mult))
                link(dve.tensor_tensor(sq1[:, t, 576:640], Z[:, t, IK1:IK1 + HD], Z[:, t, IK1:IK1 + HD], ALU.mult))
            link(dve.tensor_reduce(st1[:, 2, :], sq1.rearrange("p t (h d) -> p (t h) d", d=HD), AX_X, ALU.add))
            dve.tensor_scalar(st1[:, 0, :], st1[:, 2, :], 1.0 / HD, EPS, ALU.mult, ALU.add).then_inc(sem("qk1_meansq"), 1)
            dve.wait_ge(sem("qk1_root"), 1)
            link(dve.reciprocal(st1[:, 2, :], st1[:, 1, :]))
            for t in range(T):
                r0 = 10 * t
                dve.tensor_tensor(N1[:, t, 0:512].rearrange("p (h d) -> p h d", d=HD),
                                  Z[:, t, 0:512].rearrange("p (h d) -> p h d", d=HD),
                                  bc(st1[:, 2, r0:r0 + 8], 2, HD), ALU.mult)
                for dup in range(2):
                    dve.tensor_scalar(N1[:, t, 512 + dup * HD:576 + dup * HD], Z[:, t, K1:K1 + HD],
                                      st1[:, 2, r0 + 8:r0 + 9], None, ALU.mult)
                    dve.tensor_scalar(N1[:, t, 896 + dup * HD:960 + dup * HD], Z[:, t, IK1:IK1 + HD],
                                      st1[:, 2, r0 + 9:r0 + 10], None, ALU.mult)
                link(dve.tensor_copy(N1[:, t, 640:896], Z[:, t, IQ1:IQ1 + 256]))
            dve.memset(m8[:, :], 0.0).then_inc(sem("qk1_normed"), 1)
            keep_turned("qk1", NT1, lambda c: col("gain1", c))
            for t in range(T):
                n = (t + 1) * P
                dve.wait_ge(sem("index_products"), t + 1)
                for h in range(HI):
                    src = PS[:, 4 + 2 * t + h % 2, (h // 2) * S:(h // 2) * S + n]
                    dst = score[:, t, 0:n] if h == 0 else stmp[:, 0:n]
                    link(dve.tensor_scalar(dst, src, 0.0, Z[:, t, IW1 + h:IW1 + h + 1], ALU.max, ALU.mult))
                    if h:
                        link(dve.tensor_tensor(score[:, t, 0:n], score[:, t, 0:n], stmp[:, 0:n], ALU.add))
                link(dve.memset(score[0:HD, t, n - HD:n], BARRED))
                src = score
                for _ in range(NSEL // 8):
                    link(dve.max(m8[:, :], src[:, t, 0:n]))
                    link(dve.match_replace(work[:, t, 0:n], m8[:, :], src[:, t, 0:n], TAKEN))
                    src = work
                dve.tensor_scalar(bias1[:, t, 0:n], work[:, t, 0:n], BARRED * 2, MASKED, ALU.is_gt,
                                  ALU.mult).then_inc(sem("chosen"), 1)
            dve.wait_ge(sem("chosen"), T)
            attention("a1", HD ** -0.5)
            dve.wait_ge(sem("sig1"), T)
            wait_used(dve, "up_attn")
            wait_used(dve, "up_pool")
            for t in range(T):
                for half in range(2):
                    o = half * NB
                    link(dve.tensor_tensor(mtmp[:, 0, :], PS[:, 2 * t + half, :], Z[:, t, G1 + o:G1 + o + NB], ALU.mult))
                    link(dve.tensor_tensor(mtmp[:, 1, :], PS[:, 4 + 2 * t + half, :],
                                           Z[:, t, G1 + D + o:G1 + D + o + NB], ALU.mult))
                    link(dve.tensor_tensor(M1[:, t, o:o + NB], mtmp[:, 0, :], mtmp[:, 1, :], ALU.add))
            dve.memset(m8[:, :], 0.0).then_inc(sem("m1_ready"), 1)
            keep_turned("m1", MT1)
            dve.wait_ge(sem("gate1_kept"), 2)
            for half in range(2):
                wait_used(dve, f"out{half}")
                for t in range(T):
                    o = half * NB
                    link(dve.tensor_tensor(mtmp[:, t, :], PS[:, 4 + 2 * t + half, :], gate1[:, o:o + NB], ALU.mult))
                    dve.tensor_tensor(X[:, t, o:o + NB], X[:, t, o:o + NB], mtmp[:, t, :],
                                      ALU.add).then_inc(sem("x1_ready"), 1)
            dve.wait_ge(sem("x1_ready"), 4)
            scaled("n2", XN1)
            keep_turned("n2", hT, lambda c: adaT[:, 32 + c:33 + c], lambda c: adaT[:, 24 + c:25 + c])
            for t in range(T):
                dve.wait_ge(sem("scores_kept"), 4 * (t + 1))
                for k in range(2 * PH):
                    for rnd in range(2):
                        tv = TV[:, t, k, 8 * rnd:8 * rnd + 8]
                        link(dve.max(tv, SX[:, t, k, :]))
                        link(dve.max_index(TI[:, t, k, 8 * rnd:8 * rnd + 8].bitcast(U32), tv, SX[:, t, k, :]))
                        if rnd == 0:
                            link(dve.match_replace(SX[:, t, k, :], tv, SX[:, t, k, :], TAKEN))
            for t in range(T):
                halves = TV[:, t, :, :].rearrange("p (h w) k -> p w h k", w=2)
                link(dve.tensor_tensor(CAND.rearrange("p h (x y) -> p h x y", x=TOPK),
                                       bc(halves[:, 0], 3, TOPK), bc(halves[:, 1], 2, TOPK), ALU.add))
                for h in range(PH):
                    for rnd in range(2):
                        bv = BV[:, t, h, 8 * rnd:8 * rnd + 8]
                        link(dve.max(bv, CAND[:, h, :]))
                        link(dve.max_index(BI[:, t, h, 8 * rnd:8 * rnd + 8].bitcast(U32), bv, CAND[:, h, :]))
                        if rnd == 0:
                            link(dve.match_replace(CAND[:, h, :], bv, CAND[:, h, :], TAKEN))
            dve.tensor_tensor(BE, BV, BV[:, :, :, 0:1].broadcast_to([P, T, PH, TOPK]),
                              ALU.subtract).then_inc(sem("best_less_max"), 1)
            link(dve.tensor_copy(TI, TI.bitcast(U32)))
            for t in range(T):
                bi = BI[:, t, :, :].bitcast(U32)
                for w in range(2):
                    ab = AB[:, w, :, :].bitcast(U32)
                    if w == 0:
                        link(dve.tensor_scalar(ab, bi, 4, None, ALU.logical_shift_right))
                    else:
                        link(dve.tensor_scalar(ab, bi, TOPK - 1, None, ALU.bitwise_and))
                    link(dve.tensor_copy(AB[:, w, :, :], ab))
                    keys = TI[:, t, :, :].rearrange("p (h w) k -> p w h k", w=2)[:, w]
                    link(dve.tensor_tensor(EQ, bc(AB[:, w, :, :], 3, TOPK),
                                           bc(bc(iota[:, 0:TOPK], 1, TOPK), 1, PH), ALU.is_equal))
                    link(dve.tensor_tensor(EQ, EQ, bc(keys, 2, TOPK), ALU.mult))
                    link(dve.tensor_reduce(SLOT[:, w, t, :].rearrange("p (h k) -> p h k", h=PH), EQ, AX_X, ALU.add))
            dve.wait_ge(sem("best_exp"), 1)
            link(dve.tensor_reduce(gsum[:, 0, :], BE.rearrange("p t h k -> p (t h) k"), AX_X, ALU.add))
            link(dve.reciprocal(gsum[:, 1, :], gsum[:, 0, :]))
            dve.tensor_tensor(SLOT[:, 2, :, :].rearrange("p t (h k) -> p (t h) k", h=PH),
                              BE.rearrange("p t h k -> p (t h) k"), bc(gsum[:, 1, :], 2, TOPK),
                              ALU.mult).then_inc(sem("slots_ready"), 1)
            dve.wait_ge(sem("slots_turned"), 1)
            for w in range(3):
                dve.tensor_copy(slotT[:, w, :], PS[:, 6 + w // 2, (w % 2) * S:(w % 2 + 1) * S]).then_inc(
                    sem("slots_saved"), 1)
            dve.wait_ge(sem("slots_saved"), 3)
            dve.sem_inc(sem("gate_banks_free"), 2)

            def rows(g, r=0):
                if not (isinstance(r, int) and g < 2):
                    dve.wait_ge(sem("gates_placed"), g + 2 * r)
                for j in range(4):
                    n = bass.ds(4 * g + j + 8 * r, 1)
                    dve.tensor_scalar(onehot[:, 0, g % 2, j, :], iota[:, :], slotT[:, 0, n], None, ALU.is_equal)
                    last = dve.tensor_scalar(onehot[:, 1, g % 2, j, :], iota[:, :], slotT[:, 1, n], slotT[:, 2, n],
                                             ALU.is_equal, ALU.mult)
                last.then_inc(sem("onehot_ready"), 1)

            act_v = region[:, :].rearrange("p (i n) -> p i n", n=S)

            def weigh(g, r=0):
                dve.wait_ge(sem("gates_placed"), g + 2 + 2 * r)
                v = act_v[:, :, bass.ds(4 * g + 8 * r, 4)]
                dve.tensor_tensor(v, v, PS[:, g % 2, :].rearrange("p (n i) -> p i n", n=4),
                                  ALU.mult).then_inc(sem("gate_banks_free"), 1)

            dve.wait_ge(sem("u_banks_free"), 6 + 2 * U_BLOCKS)
            rows(0)
            with dve.Fori(0, S // 8 - 1) as r:
                rows(1, r)
                weigh(0, r)
                rows(2, r)
                weigh(1, r)
            rows(S // 4 - 1)
            weigh(S // 4 - 2)
            weigh(S // 4 - 1)
            dve.wait_ge(sem("gate_banks_free"), 2 + S // 4)
            dve.memset(tiny[:, 8:9], 0.0).then_inc(sem("weighted"), 1)
            dve.wait_ge(used[(AT["v0"] + U_BLOCKS - 1) % RING], (AT["v0"] + U_BLOCKS - 1) // RING + 1)
            for c in range(KC // 2, KC):
                dve.tensor_scalar(hT[:, c, :], PS[:, 4 + c // 2, (c % 2) * S:(c % 2 + 1) * S], adaT[:, 40 + c:41 + c],
                                  None, ALU.mult).then_inc(sem("peer_out_kept"), 1)
            for t in range(T):
                for half in range(2):
                    dve.wait_ge(sem("peer_out_turned"), 2 * t + half + 1)
                    xs = X[:, t, half * NB:(half + 1) * NB]
                    dve.tensor_tensor(xs, xs, PS[:, 2 * t + half, :], ALU.add).then_inc(sem("x2_ready"), 1)

            dve.wait_ge(sem("x2_ready"), 4)
            scaled("n3", XN2)
            lam = cols[0:RW, COL["lam"][0]:COL["lam"][0] + RB]
            s = [sp[0:RW, i, :] for i in range(8)]
            link(dve.tensor_scalar(s[2], lam, -1.0, None, ALU.mult))
            dve.tensor_tensor(s[0], lam, s[2], ALU.max).then_inc(sem("lam_abs"), 1)
            dve.wait_ge(sem("lam_exp"), 1)
            link(dve.tensor_scalar(s[3], s[1], 2.0, None, ALU.add))
            link(dve.reciprocal(s[4], s[3]))
            link(dve.tensor_tensor(s[5], s[1], s[4], ALU.mult))
            link(dve.tensor_tensor(s[6], s[5], s[5], ALU.mult))
            link(dve.tensor_scalar(s[7], s[6], 1.0 / 15, 1.0 / 13, ALU.mult, ALU.add))
            for k in (11, 9, 7, 5, 3, 1):
                link(dve.tensor_tensor(s[7], s[7], s[6], ALU.mult))
                link(dve.tensor_scalar(s[7], s[7], 1.0 / k, None, ALU.add))
            link(dve.tensor_tensor(s[7], s[7], s[5], ALU.mult))
            link(dve.tensor_scalar(s[7], s[7], 8.0, None, ALU.mult))
            link(dve.tensor_scalar(s[2], s[2], 0.0, 4.0, ALU.max, ALU.mult))
            dve.tensor_tensor(s[7], s[7], s[2], ALU.add).then_inc(sem("decay_ready"), 1)
            keep_turned("n3", hT, lambda c: col("n1", c))
            for n in range(RB):
                dve.wait_ge(sem("r_kept"), n + 1)
                link(dve.tensor_scalar(XC[0:RW, n, :], RX[0:RW, n, :], col("cw", 3 * RB + n, RW), col("cb", n, RW),
                                       ALU.mult, ALU.add))
                for k in (1, 2, 3):
                    ins = dve.scalar_tensor_tensor(XC[0:RW, n, k:S], RX[0:RW, n, 0:S - k],
                                                   col("cw", (3 - k) * RB + n, RW), XC[0:RW, n, k:S],
                                                   ALU.mult, ALU.add)
                    if k < 3:
                        link(ins)
                ins.then_inc(sem("conv_done"), 1)

            def flat(b):
                return b[0:RW, :, :].rearrange("p b s -> p (b s)")

            dve.wait_ge(sem("conv_done"), RB)
            dve.wait_ge(sem("rgate_kept"), 2 * RB)
            dve.tensor_tensor(flat(IT), flat(IT), flat(XC), ALU.mult).then_inc(sem("xc_used"), 1)
            dve.wait_ge(sem("xc_used"), 1)
            dve.wait_ge(sem("tanh_done"), RB)
            link(dve.tensor_scalar(flat(RX), flat(RT), 1.0, None, ALU.add))
            link(dve.reciprocal(flat(RX), flat(RX)))
            dve.wait_ge(sem("root_tanh"), 1)
            link(dve.tensor_tensor(flat(XC), flat(XC), flat(RX), ALU.mult))
            link(dve.scalar_tensor_tensor(flat(IT), flat(XC), 2.0, flat(IT), ALU.mult, ALU.mult))
            link(dve.tensor_scalar(flat(RT), flat(RX), 2.0, -1.0, ALU.mult, ALU.add))
            for n in range(RB):
                ins = dve.tensor_tensor_scan(XC[0:RW, n, :], RT[0:RW, n, :], IT[0:RW, n, :], 0.0, ALU.mult, ALU.add)
            link(ins)
            dve.wait_ge(sem("r_kept"), 2 * RB)
            dve.tensor_tensor(flat(XC), flat(XC), flat(RGT), ALU.mult).then_inc(sem("rec_out"), 1)
            dve.wait_ge(sem("rec_out"), 1)
            dve.wait_ge(sem("sq2"), 3 * T)
            link(dve.tensor_reduce(st2[:, 2, :], SQ2.rearrange("p t (h d) -> p (t h) d", d=HD), AX_X, ALU.add))
            dve.tensor_scalar(st2[:, 0, :], st2[:, 2, :], 1.0 / HD, EPS, ALU.mult, ALU.add).then_inc(sem("qk2_meansq"), 1)
            dve.wait_ge(sem("qk2_root"), 1)
            link(dve.reciprocal(st2[:, 2, :], st2[:, 1, :]))
            for t in range(T):
                link(dve.tensor_tensor(N2[:, t, :].rearrange("p (h d) -> p h d", d=HD),
                                       Z2[:, t, 0:D].rearrange("p (h d) -> p h d", d=HD),
                                       bc(st2[:, 2, 24 * t:24 * t + 16], 2, HD), ALU.mult))
            dve.memset(PEB[:, :], 0.0).then_inc(sem("q2_normed"), 1)
            keep_turned("q2", QT2, lambda c: col("gainq"))
            for t in range(T):
                for w, o in enumerate((KS2, KW2)):
                    for dup in range(2):
                        dst = N2[:, t, w * 512:(w + 1) * 512].rearrange("p (g e d) -> p g e d", g=KV, e=2)[:, :, dup, :]
                        link(dve.tensor_tensor(dst, Z2[:, t, o:o + 256].rearrange("p (g d) -> p g d", g=KV),
                                               bc(st2[:, 2, 24 * t + 16 + 4 * w:24 * t + 20 + 4 * w], 2, HD), ALU.mult))
            dve.memset(PEB[:, :], 0.0).then_inc(sem("k2_normed"), 1)
            keep_turned("k2", KT2, lambda c: col("gainkw"))
            for t in range(T):
                for w, o in enumerate((KC2, VC2)):
                    for dup in range(2):
                        dst = N2[:, t, w * 512:(w + 1) * 512].rearrange("p (g e d) -> p g e d", g=KV, e=2)[:, :, dup, :]
                        link(dve.tensor_copy(dst, Z2[:, t, o:o + 256].rearrange("p (g d) -> p g d", g=KV)))
            dve.memset(HID[:, :, :], 0.0).then_inc(sem("c2_copied"), 1)
            for c in range(KC // 2, KC):
                dve.wait_ge(sem("c2_turned"), c // 2 + 1)
                src = PS[:, c // 2, (c % 2) * S:(c % 2 + 1) * S]
                dve.tensor_copy(CT2[0:HD, c, :], src[0:HD, :]).then_inc(sem("c2_kept"), 1)
                dve.tensor_copy(CT2[HD:P, c, 0:S - 1], src[HD:P, 1:S]).then_inc(sem("c2_kept"), 1)
            wait_used(dve, "cmp")
            dve.wait_ge(sem("c2_copied"), 1)
            dve.tensor_copy(PEB[:, :], PS[:, 2:4, 0:1].rearrange("p a b -> p (a b)")).then_inc(sem("pe_bias"), 1)
            dve.wait_ge(sem("cmp_made"), 1)
            link(dve.tensor_copy(kcmp[0:HD, 0, 0:HD], PS[0:HD, 0, 128:128 + HD]))
            link(dve.tensor_copy(vcmp, PS[:, 1, 128:128 + HD]))
            link(dve.tensor_tensor(kcmp[0:HD, 0, HD:P], kcmp[0:HD, 0, 0:HD], kcmp[0:HD, 0, 0:HD], ALU.mult))
            link(dve.tensor_reduce(cst[0:HD, 0, 1:2], kcmp[0:HD, 0, HD:P], AX_X, ALU.add))
            dve.tensor_scalar(cst[0:HD, 0, 0:1], cst[0:HD, 0, 1:2], 1.0 / HD, EPS, ALU.mult,
                              ALU.add).then_inc(sem("kcmp_meansq"), 1)
            dve.wait_ge(sem("kcmp_root"), 1)
            link(dve.reciprocal(cst[0:HD, 0, 2:3], cst[0:HD, 1, 0:1]))
            link(dve.tensor_scalar(kcmp[0:HD, 1, 0:HD], kcmp[0:HD, 0, 0:HD], cst[0:HD, 0, 2:3], None, ALU.mult))
            dve.tensor_scalar(kcmp[0:HD, 1, HD:P], kcmp[0:HD, 0, 0:HD], cst[0:HD, 0, 2:3], None,
                              ALU.mult).then_inc(sem("kcmp_normed"), 1)
            dve.wait_ge(sem("kcmp_turned"), 1)
            dve.tensor_scalar(kcmp[:, 2, 0:HD], PS[:, 2, 0:HD], col("gainkc"), None,
                              ALU.mult).then_inc(sem("kcmp_kept"), 1)
            wait_used(dve, "ro3")
            dve.wait_ge(sem("sig2"), T)
            dve.wait_ge(sem("n3_turned"), KC // 2)
            for t in range(T):
                for half in range(2):
                    o = half * NB
                    dve.tensor_tensor(M2[:, t, o:o + NB], PS[:, 4 + 2 * t + half, :], Z2[:, t, MR2 + o:MR2 + o + NB],
                                      ALU.mult).then_inc(sem("rec_gated"), 1)
            dve.wait_ge(sem("consts2_loaded"), 16)
            dve.wait_ge(sem("cmp_logits"), 1)
            for t in range(T):
                l3 = LC[:, t, :].rearrange("p (h i) -> p h i", h=H2)
                for e in range(2):
                    p3 = PS[:, 3 * e, t * P:(t + 1) * P].rearrange("p (h i) -> p h i", h=H2 // 2)
                    link(dve.scalar_tensor_tensor(l3[:, e:H2:2, :], p3, HD ** -0.5, bc(cneg[:, t, :], 1, H2 // 2),
                                                  ALU.mult, ALU.add))
                link(dve.tensor_reduce(cst[:, 2, t * 16:(t + 1) * 16], l3, AX_X, ALU.max))
                link(dve.tensor_tensor(l3, l3, bc(cst[:, 2, t * 16:(t + 1) * 16], 2, 16), ALU.subtract))
            dve.memset(cst[:, 1, :], 0.0).then_inc(sem("cmp_less_max"), 1)
            dve.wait_ge(sem("c2_turned"), KC // 2)
            link(dve.memset(PZ, 0.0))
            dve.wait_ge(sem("cmp_exp"), 1)
            for t in range(T):
                l3 = LC[:, t, :].rearrange("p (h i) -> p h i", h=H2)
                link(dve.tensor_reduce(cst[:, 2, t * 16:(t + 1) * 16], l3, AX_X, ALU.add))
                link(dve.reciprocal(cst[:, 3, t * 16:(t + 1) * 16], cst[:, 2, t * 16:(t + 1) * 16]))
                link(dve.tensor_tensor(cst[:, 3, t * 16:(t + 1) * 16], cst[:, 3, t * 16:(t + 1) * 16],
                                       NSG[:, t, 0:48:3], ALU.mult))
                link(dve.tensor_tensor(l3, l3, bc(c01[:, t, :], 1, H2), ALU.mult))
                link(dve.tensor_tensor(l3, l3, bc(cst[:, 3, t * 16:(t + 1) * 16], 2, 16), ALU.mult))
                pz = PZ[:, t, :].rearrange("p (h k) -> p h k", h=H2)
                for g in range(KV):
                    link(dve.tensor_copy(pz[:, 4 * g:4 * g + 4, 16 * g:16 * g + 16], l3[:, 4 * g:4 * g + 4, :]))
            dve.memset(cst[:, 1, :], 0.0).then_inc(sem("cmp_probs"), 1)
            keep_turned("pz", PZT)
            attention("a2", HD ** -0.5)
            wait_used(dve, "ao1")
            for t in range(T):
                for half in range(2):
                    o = half * NB
                    link(dve.tensor_tensor(f2[:, half, :], PS[:, 2 * t + half, :], Z2[:, t, MA2 + o:MA2 + o + NB], ALU.mult))
                    dve.tensor_tensor(M2[:, t, o:o + NB], M2[:, t, o:o + NB], f2[:, half, :],
                                      ALU.add).then_inc(sem("m2_ready"), 1)
            keep_turned("m2", MT2)
            for half in range(2):
                wait_used(dve, f"oo{half}")
                for t in range(T):
                    xs = X[:, t, half * NB:(half + 1) * NB]
                    dve.tensor_tensor(xs, xs, PS[:, 4 + 2 * t + half, :], ALU.add).then_inc(sem("x3_ready"), 1)
            dve.wait_ge(sem("x3_ready"), 4)
            scaled("n4", XN4)
            keep_turned("n4", hT, lambda c: col("n2", c))
            for f in range(F_B):
                for w, (name, buf) in enumerate((("fg", CG), ("fv", CV))):
                    wait_used(dve, f"{name}{f}")
                    for q in range(4):
                        i = w * FT + 4 * f + q
                        src = PS[:, 4 * (f % 2) + 2 * w + q // 2, (q % 2) * S:(q % 2 + 1) * S]
                        if w == 0 and f:
                            dve.wait_ge(sem("ffn_gated"), 4 * (f - 1) + q + 1)
                        link(dve.tensor_scalar(buf[:, q, :], src, col("ffw", 2 * 2 * FT + i), col("ffb", i),
                                               ALU.mult, ALU.add))
                        link(dve.scalar_tensor_tensor(buf[:, q, 1:S], src[:, 0:S - 1], col("ffw", 2 * FT + i),
                                                      buf[:, q, 1:S], ALU.mult, ALU.add))
                        dve.scalar_tensor_tensor(buf[:, q, 2:S], src[:, 0:S - 2], col("ffw", i), buf[:, q, 2:S],
                                                 ALU.mult, ALU.add).then_inc(sem(f"{name}_read"), 1)
                        dve.wait_ge(sem(f"{name}_read"), 4 * f + q + 1)
                        if w == 0:
                            dve.sem_inc(sem("fg_conv"), 1)
                        else:
                            dve.wait_ge(sem("fg_gelu"), 4 * f + q + 1)
                            dve.tensor_tensor(GV[:, 4 * f + q, :], CG[:, q, :], CV[:, q, :],
                                              ALU.mult).then_inc(sem("ffn_gated"), 1)
            wait_used(dve, "dn5")
            for t in range(T):
                for half in range(2):
                    xs = X[:, t, half * NB:(half + 1) * NB]
                    dve.tensor_tensor(xs, xs, PS[:, 2 * t + half, :], ALU.add).then_inc(sem("result_ready"), 1)


def lay_out(v):
    f = np.float32

    def kblocks(w, cuts):
        k = w.shape[0] // P
        w3 = w.reshape(k, P, w.shape[1])
        res = []
        for idx in cuts:
            blk = np.zeros((P, k, BLK // k), f)
            blk[:, :, :len(idx)] = w3[:, :, idx].transpose(1, 0, 2)
            res.append(blk.reshape(P, BLK))
        return res

    def ranges(n, w=NB):
        return [np.arange(i, min(i + w, n)) for i in range(0, n, w)]

    def rows4(w):
        k = w.shape[0] // P
        return [w.reshape(k, P, D)[4 * i:4 * i + 4].transpose(1, 0, 2).reshape(P, BLK) for i in range(k // 4)]

    blocks = {}

    def put(prefix, lst):
        for i, b in enumerate(lst):
            blocks[f"{prefix}{i}"] = b

    put("ada", kblocks(v["w_ada"][0], ranges(6 * D)))
    put("in", kblocks(v["w_in"][0], ranges(Z1W)))
    blocks["up_attn"] = rows4(v["w_up_attn"][0])[0]
    blocks["up_pool"] = rows4(v["w_up_pool"][0])[0]
    put("out", kblocks(v["w_out"][0], ranges(D)))
    put("pq", kblocks(v["w_peer_q"][0], ranges(D)))
    w2 = v["w_in_2"]
    rnn = 2 * RB * RW
    nsa = rnn + H2 * HD + 6 * KV * HD
    cuts = ranges(rnn, SUB * RW)
    cuts[-1] = np.concatenate([cuts[-1], np.arange(nsa, nsa + 48)])
    put("r", kblocks(w2, cuts))
    rest = np.concatenate([np.arange(rnn, nsa), np.arange(nsa + 48, w2.shape[1])])
    put("z", kblocks(w2, [rest[i] for i in ranges(Z2W)]))
    rg = np.zeros((P, BLK), f)
    rg[:RW, :2 * RB * RW] = np.stack([v["rg_w_a_2"], v["rg_w_x_2"]]).transpose(2, 0, 1, 3).reshape(RW, -1)
    blocks["rgate"] = rg
    cmp_w = np.stack([v["cmp_w1_k_2"], v["cmp_w1_v_2"]]).reshape(2, CLEN // 2, P, P)
    blocks["cmp"] = cmp_w.transpose(2, 0, 1, 3).reshape(P, BLK)
    ro = np.zeros((4, P, 4, D), f)
    ro[:, :RW] = v["w_rnn_out_2"].reshape(4, 4, RW, D).transpose(0, 2, 1, 3)
    put("ro", list(ro.reshape(4, P, BLK)))
    put("ao", kblocks(v["w_attn_out_2"], ranges(D)))
    put("oo", kblocks(v["w_out_2"], ranges(D)))
    put("fg", kblocks(v["w_up_2"][:, :FF], ranges(FF)))
    put("fv", kblocks(v["w_up_2"][:, FF:], ranges(FF)))
    put("dn", rows4(v["w_down_2"]))
    stream = np.empty((len(ORDER), P, BLK), f)
    for n, b in blocks.items():
        stream[AT[n]] = b
    u = v["peer_u"][0].reshape(NK, U_BLOCKS, I2_PER, KC, P)
    stream[AT["u0"]:AT["u0"] + U_BLOCKS] = u.transpose(1, 4, 2, 3, 0).reshape(U_BLOCKS, P, BLK)
    vv = v["peer_v"][0].reshape(NK, U_BLOCKS, I2_PER * D)
    stream[AT["v0"]:AT["v0"] + U_BLOCKS] = vv.transpose(1, 0, 2)

    cols = np.zeros((P, NCOL), f)

    def place(name, m):
        o = COL[name][0]
        assert m.shape[1] == COL[name][1], name
        cols[:m.shape[0], o:o + m.shape[1]] = m

    def feat(x):
        return x.reshape(-1, P).T

    twice = lambda x: np.concatenate([x, x])[:, None]
    place("cT", feat(v["c"][0]))
    place("g1", feat(v["g_norm1"][0]))
    place("g2", feat(v["g_norm2"][0]))
    place("bada", feat(v["b_ada"][0]))
    gq, gk, gi = twice(v["g_q"][0]), twice(v["g_k"][0]), twice(v["g_ik"][0])
    one = np.ones((P, 1), f)
    place("gain1", np.concatenate([gq] * 4 + [gk, one, one, gi], axis=1))
    place("spool", v["s_pool"][0].T)
    place("n1", feat(v["norm1_g_2"]))
    place("n2", feat(v["norm2_g_2"]))
    place("gainq", twice(v["q_norm_g_2"]))
    place("gainks", twice(v["k_slc_norm_g_2"]))
    place("gainkw", twice(v["k_win_norm_g_2"]))
    place("gainkc", twice(v["k_cmp_norm_g_2"]))
    place("pek", v["cmp_pe_k_2"].reshape(CLEN // 2, P).T)
    place("pev", v["cmp_pe_v_2"].reshape(CLEN // 2, P).T)
    place("ffw", np.concatenate([feat(v["ffn_conv_w_2"][k]) for k in range(3)], axis=1))
    place("ffb", feat(v["ffn_conv_b_2"]))
    place("ba", v["rg_b_a_2"].reshape(RB, RW).T)
    place("bx", v["rg_b_x_2"].reshape(RB, RW).T)
    place("lam", v["lru_lambda_2"].reshape(RB, RW).T)
    place("cw", np.concatenate([v["rnn_conv_w_2"][k].reshape(RB, RW).T for k in range(4)], axis=1))
    place("cb", v["rnn_conv_b_2"].reshape(RB, RW).T)

    consts = np.concatenate([np.eye(P), np.tile(np.arange(P), (P, 1)), np.ones((P, P))], axis=1).astype(f)
    s, t = np.arange(S)[:, None], np.arange(S)[None, :]
    band = np.stack([((s <= t) & (s > t - w)) / np.minimum(t + 1, w) - (s == t) for w in (2, 4, 8, 16)])
    band = band.reshape(4, T, P, S).transpose(2, 1, 0, 3).reshape(P, -1).astype(f)
    q = np.arange(S)
    causal = np.where(np.arange(S)[None] <= q[:, None], 0.0, MASKED).reshape(T, P, S).transpose(1, 0, 2).reshape(P, -1)
    i = np.arange(16)
    ok = (i[None] < NCMP) & (i[None] * CSTEP + CLEN - 1 <= q[:, None])
    ok = ok.reshape(T, P, 16).transpose(1, 0, 2).reshape(P, -1)
    consts2 = np.concatenate([causal.astype(f), np.where(ok, 0.0, MASKED).astype(f), ok.astype(f),
                              v["cmp_w2_k_2"], v["cmp_w2_v_2"]], axis=1)
    return {
        "x": v["x"][0], "stream": stream, "cols": cols, "consts": consts, "consts2": consts2, "band": band,
        "brow": v["b_ada"][0][None, 2 * D:3 * D], "wpool": v["w_pool_grp"][0].transpose(1, 0, 2).reshape(P, -1),
        "skeys": v["peer_subkeys"][0].transpose(1, 3, 0, 2).reshape(P, -1),
    }


def kernel(**inputs):
    import concourse.bacc as _bacc
    from concourse.bass_utils import run_bass_kernel_spmd as _run

    nc = _bacc.Bacc("TRN2", target_bir_lowering=False, num_devices=1)
    arrays = {n: np.ascontiguousarray(x) for n, x in lay_out({k: np.asarray(x) for k, x in inputs.items()}).items()}
    aps = {n: nc.dram_tensor(f"in_{n}", x.shape, mybir.dt.from_np(x.dtype), kind="ExternalInput").ap()
           for n, x in arrays.items()}
    out = nc.dram_tensor("result", (S, D), F32, kind="ExternalOutput").ap()
    build_program(nc, aps, out)
    r = _run(nc, [{f"in_{n}": x for n, x in arrays.items()}], core_ids=[0])
    return r.results[0]["result"].reshape(1, S, D)
```

```python
from contextlib import ExitStack

import numpy as np

import concourse.bass as bass
from concourse import mybir
from concourse.alu_op_type import AluOpType as ALU

ACT = mybir.ActivationFunctionType
F32 = mybir.dt.float32
F32R = mybir.dt.float32r
U32 = mybir.dt.uint32
AX_X = mybir.AxisListType.X

P = 128
S = 256
T = S // P
D = 1024
KC = D // P
NB = 512
BLK = KC * NB
QUARTERS = 4
QUARTER = BLK // QUARTERS
RING = 4
EPS = 1e-6
HD = 64
MASKED = -1e30
BARRED = -1e38
TAKEN = -3e38

H1, HI = 8, 4
Q1, K1, V1, IQ1 = 0, 512, 576, 640
IK1 = IQ1 + HI * HD
IW1 = IK1 + HD
P1 = IW1 + HI
G1 = P1 + 512
Z1W = 3524
Z1B = -(-Z1W // NB)
NSEL = 64
ADA_B = 6 * D // NB
ADA_DVE = 10
PH, NK, TOPK = 8, 128, 16
SLOTS = PH * TOPK
I2_PER = 4
U_BLOCKS = NK // I2_PER
RB, RW = 16, 84
R_BLOCKS = 2 * RB // QUARTERS
GATES = 48
H2, KV = 16, 4
KC2, VC2, KS2, VS2, KW2, VW2, MR2, MA2 = 1024, 1280, 1536, 1792, 2048, 2304, 2560, 3584
Z2W = 4608
Z2B = Z2W // NB
NCMP, CSTEP, CLEN = 15, 16, 32
FF = 3072
FT = FF // P
F_B = FF // NB

_COLS = [("cT", 8), ("g1", 8), ("g2", 8), ("bada", 48), ("gain1", 8), ("spool", 4), ("n1", 8), ("n2", 8),
         ("gainq", 1), ("gainks", 1), ("gainkw", 1), ("gainkc", 1), ("pek", 16), ("pev", 16),
         ("ffw", 3 * 2 * FT), ("ffb", 2 * FT), ("ba", RB), ("bx", RB), ("lam", RB), ("cw", 4 * RB), ("cb", RB)]
COL = {}
_at = 0
for _n, _w in _COLS:
    COL[_n] = (_at, _w)
    _at += _w
NCOL = _at


def plan():
    order = [f"ada{j}" for j in range(4)]
    for i in range(Z1B):
        order += [f"in{i}"] + [f"ada{j}" for j in [i + 3] if 4 <= j < ADA_DVE]
    order += [f"ada{j}" for j in range(ADA_DVE, ADA_B)]
    order += ["up_attn", "up_pool", "out0", "out1", "pq0", "pq1"]
    order += [f"u{m}" for m in range(U_BLOCKS)] + [f"v{m}" for m in range(U_BLOCKS)]
    order += [f"r{i}" for i in range(R_BLOCKS)] + ["z0", "z1", "rgate"] + [f"z{i}" for i in range(2, Z2B)]
    order += ["cmp"] + [f"ro{i}" for i in range(4)] + ["ao0", "ao1", "oo0", "oo1"]
    for f in range(F_B):
        order += [f"fg{f}", f"fv{f}"]
    return order + [f"dn{i}" for i in range(6)]


ORDER = plan()
AT = {n: i for i, n in enumerate(ORDER)}
N_QUARTERS = QUARTERS * len(ORDER)
PAIRED = {f"in{i}": f"ada{i + 3}" for i in range(Z1B) if 4 <= i + 3 < ADA_DVE}


def quarter_no(name, q):
    if name in PAIRED:
        return QUARTERS * AT[name] + 2 * q
    if name in PAIRED.values():
        return QUARTERS * (AT[name] - 1) + 2 * q + 1
    return QUARTERS * AT[name] + q


NAME_AT = {quarter_no(n, q): n for n in ORDER for q in range(QUARTERS)}
SPLIT = [NAME_AT[b].rstrip("0123456789") in ("in", "pq", "u", "v", "r", "z", "ro", "fg", "fv",
                                                "dn") for b in range(N_QUARTERS)]


def nth_split(b):
    return sum(SPLIT[i] for i in range(b % RING, b + 1, RING))


def build_program(nc, a, out):
    ctx = ExitStack()
    with ctx:
        names = {}

        def sem(name):
            if name not in names:
                names[name] = ctx.enter_context(nc.semaphore(name))
            return names[name]

        def sb(name, shape, dt=F32):
            return ctx.enter_context(nc.sbuf_tensor(name, shape, dt))

        class Pair(tuple):

            def __getitem__(self, key):
                return Pair(x[key] for x in self)

            def rearrange_all(self, inner):
                return Pair(x.rearrange("p (c n) -> p c n", n=inner) for x in self)

        region = sb("region", [P, NK * S])
        ring = sb("ring", [P, RING, QUARTER])
        high = sb("high", [P, RING, QUARTER], F32R)
        low = sb("low", [P, RING, QUARTER], F32R)
        X = sb("X", [P, T, D])
        hTh = sb("hTh", [P, KC, S], F32R)
        hTl = sb("hTl", [P, KC, S], F32R)
        ident = sb("ident", [P, P])
        iota = sb("iota", [P, P])
        ones = sb("ones", [P, P])
        cols = sb("cols", [P, NCOL])
        slotT = sb("slotT", [P, 3, S])
        adaT = sb("adaT", [P, 48])
        tiny = sb("tiny", [P, 64])
        PS = ctx.enter_context(nc.psum_tensor("PS", [P, 8, NB], F32))

        def col(name, i=0, n=P):
            o = COL[name][0] + i
            return cols[0:n, o:o + 1]

        def carve(start):
            at = [start]

            def take(*shape):
                n = int(np.prod(shape))
                v = region[:, at[0]:at[0] + n]
                at[0] += n
                assert at[0] <= NK * S, at[0]
                if len(shape) == 2:
                    v = v.rearrange("p (a b) -> p a b", a=shape[0])
                if len(shape) == 3:
                    v = v.rearrange("p (a b c) -> p a b c", a=shape[0], b=shape[1])
                if len(shape) == 4:
                    v = v.rearrange("p (a b c d) -> p a b c d", a=shape[0], b=shape[1], c=shape[2])
                return v
            return take

        take = carve(0)
        acc = take(2, NB)
        gate1 = take(D)
        XN1 = take(T, D)
        Z = take(T, Z1B * NB)
        N1 = take(T, D)
        NT1 = take(KC, S)
        band = take(T, 4, S)
        wpool = take(4, P)
        SK = take(PH, NK)
        brow = take(D)
        sq1 = take(T, 640)
        st1 = take(3, 2 * 10)
        score = take(T, S)
        work = take(T, S)
        stmp = take(S)
        m8 = take(8)
        bias1 = take(T, S)
        LB1 = take(3, S)
        PT1 = take(3, T, P)
        asm1 = take(4, 4)
        mixT = take(4, S)
        poolT = take(4, S)
        OT1 = take(4, S)
        late_acc = take(ADA_B - 4, NB)
        ada_part = acc
        M1, MT1 = N1, NT1
        mtmp = sq1.rearrange("p t n -> p (t n)")[:, 0:2 * NB].rearrange("p (t n) -> p t n", t=2)
        U_EARLY = 80
        take = carve(U_EARLY * S)
        SX = take(T, 2 * PH, NK)
        EQ = SX.rearrange("p t k n -> p (t k n)")[:, 0:PH * TOPK * TOPK].rearrange(
            "p (h k c) -> p h k c", h=PH, k=TOPK)
        TV = take(T, 2 * PH, TOPK)
        TI = take(T, 2 * PH, TOPK)
        CAND = take(PH, TOPK * TOPK)
        BV = take(T, PH, TOPK)
        BI = take(T, PH, TOPK)
        AB = take(2, PH, TOPK)
        BE = take(T, PH, TOPK)
        gsum = take(2, T * PH)
        SLOT = take(3, T, SLOTS)
        QTP = M1.rearrange("p t d -> p (t d)").rearrange("p (c s) -> p c s", c=KC)
        onehot = X[:, :, :].rearrange("p t d -> p (t d)").rearrange("p (w g j k) -> p w g j k", w=2, g=2, j=4)
        take = carve(0)
        Z2 = take(T, Z2W)
        C2 = take(704)
        NSG = take(T, 48)
        XN2 = take(T, D)
        RX = take(RB, S)
        RGT = take(RB, S)
        XC = take(RB, S)
        RT = take(RB, S)
        IT = take(RB, S)
        sp = take(8, RB)
        M2 = XN2
        base = T * Z2W + 704 + T * 48 + T * D
        take = carve(base)
        N2 = take(T, D)
        QT2 = take(KC, S)
        KT2 = take(KC, S)
        CT2 = take(KC, S)
        take = carve(base + 3 * RB * S)
        SQ2 = take(T, 1536)
        st2 = take(3, 48)
        HID = take(2, P)
        kcmp = take(3, P)
        vcmp = take(HD)
        LC = take(T, S)
        cst = take(4, 32)
        PEB = take(2)
        LB2 = take(3, S)
        PT2 = take(3, T, P)
        asm2 = take(4, 4)
        f2 = take(2, NB)
        PZ = N2
        PZT = CT2
        OT2 = RX.rearrange("p b s -> p (b s)")[:, 0:0 + 2048].rearrange("p (c s) -> p c s", c=KC)
        MT2 = QT2
        take = carve(0)
        GV = take(FT, S)
        CG = take(4, S)
        CV = take(4, S)
        XN4 = XN2
        staged = Pair((hTh[:, 0:4, :], hTl[:, 0:4, :]))
        causal = C2[:, 0:512].rearrange("p (t s) -> p t s", t=T)
        cneg = C2[:, 512:544].rearrange("p (t s) -> p t s", t=T)
        c01 = C2[:, 544:576].rearrange("p (t s) -> p t s", t=T)
        w2k, w2v = C2[:, 576:640], C2[:, 640:704]

        loaded = [sem(f"quarter_loaded{i}") for i in range(RING)]
        left = [sem(f"quarter_left_ring{i}") for i in range(RING)]
        rounded = [sem(f"quarter_rounded{i}") for i in range(RING)]
        multiplied = [sem(f"quarter_multiplied{i}") for i in range(RING)]

        def wait_loaded(eng, name, q):
            b = quarter_no(name, q)
            eng.wait_ge(loaded[b % RING], 16 * (b // RING + 1))

        def wait_split(eng, b, r=0):
            eng.wait_ge(left[b % RING], b // RING + 1 + r)

        def wait_used(eng, name, q=QUARTERS - 1):
            b = quarter_no(name, q)
            if SPLIT[b]:
                eng.wait_ge(multiplied[b % RING], nth_split(b))
            else:
                eng.wait_ge(left[b % RING], b // RING + 1)

        def slot(name, q, inner=NB):
            b = quarter_no(name, q)
            if not SPLIT[b]:
                return ring[:, b % RING, :].rearrange("p (c n) -> p c n", n=inner)
            return parts(b).rearrange_all(inner)

        def parts(b):
            return Pair((high[:, b % RING, :], low[:, b % RING, :]))

        def product(pe, out_, stat, mov, start, stop, **kw):
            if not isinstance(stat, Pair):
                return pe.matmul(out_, stat, mov, start=start, stop=stop, **kw)
            (sh, sl), (mh, ml) = tuple(stat), tuple(mov)
            pe.matmul(out_, sh, mh, start=start, stop=False, **kw)
            pe.matmul(out_, sh, ml, start=False, stop=False, **kw)
            return pe.matmul(out_, sl, mh, start=False, stop=stop, **kw)

        hT = Pair((hTh[:, :, :], hTl[:, :, :]))
        normed1 = Z[:, 0, 0:KC * S].rearrange("p (c s) -> p c s", c=KC)
        normed2 = RX.rearrange("p b s -> p (b s)")[:, 0:KC * S].rearrange("p (c s) -> p c s", c=KC)

        def ada_acc(j):
            return acc[:, j % 2, :] if j < 4 else late_acc[:, j - 4, :]

        def free_slot(name, q, ins):
            b = quarter_no(name, q)
            ins.then_inc((multiplied if SPLIT[b] else left)[b % RING], 1)

        def units1():
            for t in range(T):
                for h in range(H1):
                    lo = HD * (h % 2)
                    yield dict(q=NT1[lo:lo + HD, h // 2, t * P:(t + 1) * P],
                               k=NT1[lo:lo + HD, 4, 0:(t + 1) * P], n=t + 1, mask=bias1[:, t, 0:(t + 1) * P],
                               v=[Z[:, j, V1:V1 + HD] for j in range(t + 1)], gate=None,
                               out=PS[lo:lo + HD, 4 + h // 4, (h // 2 % 2) * S + t * P:(h // 2 % 2) * S + (t + 1) * P],
                               start=True)

        def units2():
            for br, (ko, vo) in enumerate(((0, VS2), (4, VW2))):
                for t in range(T):
                    for h in range(H2):
                        lo, g, hp = HD * (h % 2), h // (H2 // KV), h // 2
                        yield dict(q=QT2[lo:lo + HD, hp, t * P:(t + 1) * P],
                                   k=KT2[lo:lo + HD, ko + g, 0:(t + 1) * P], n=t + 1,
                                   mask=causal[:, t, 0:(t + 1) * P],
                                   v=[Z2[:, j, vo + g * HD:vo + (g + 1) * HD] for j in range(t + 1)],
                                   gate=NSG[:, t, 3 * h + 1 + br:3 * h + 2 + br],
                                   out=PS[lo:lo + HD, 4 + hp // 2, (hp % 2) * S + t * P:(hp % 2) * S + (t + 1) * P],
                                   start=False)

        ATTN = {"a1": (list(units1()), LB1, PT1, asm1), "a2": (list(units2()), LB2, PT2, asm2)}

        block = ctx.enter_context(nc.Block())

        @block.sync
        def _(sp_):
            small = sem("small_loaded")
            quarters = a["stream"].rearrange("b q p n -> (b q) p n")

            def quarter_ap(b):
                return quarters[b]

            sp_.dma_start(X[:, :, :], a["x"].rearrange("(t p) d -> p t d", p=P)).then_inc(small, 16)
            sp_.dma_start(cols[:, :], a["cols"]).then_inc(small, 16)
            sp_.dma_start(ident[:, :], a["consts"][:, 0:P]).then_inc(small, 16)
            sp_.dma_start(ones[:, :], a["consts"][:, 2 * P:3 * P]).then_inc(small, 16)
            for b in range(RING):
                sp_.dma_start(ring[:, b, :], quarter_ap(b)).then_inc(loaded[b], 16)
            n = N_QUARTERS // RING
            with sp_.Fori(1, n) as r:
                for i in range(RING):
                    sp_.wait_ge(left[i], r)
                    sp_.dma_start(ring[:, i, :], quarters[bass.ds(r * RING + i, 1)].rearrange(
                        "a p n -> p (a n)")).then_inc(loaded[i], 16)
            for b in range(n * RING, N_QUARTERS):
                sp_.wait_ge(left[b % RING], b // RING)
                sp_.dma_start(ring[:, b % RING, :], quarter_ap(b)).then_inc(loaded[b % RING], 16)
            sp_.wait_ge(sem("result_ready"), 4)
            sp_.dma_start(out.rearrange("(t p) d -> p t d", p=P), X[:, :, :]).then_inc(sem("x_moved"), 16)
            sp_.wait_ge(sem("x_moved"), 48)

        SMALL_ALL, LATER_ALL = 16 * 4, 16 * 5

        @block.tensor
        def _(pe):
            def transposes(tag, src, ready, n_ready):
                pe.wait_ge(sem(ready), n_ready)
                for c in range(KC):
                    for t in range(T):
                        last = pe.transpose(PS[:, c // 2, (c % 2) * S + t * P:(c % 2) * S + (t + 1) * P],
                                            src[:, t, c * P:(c + 1) * P], ident[:, :])
                    if c % 2:
                        last.then_inc(sem(f"{tag}_turned"), 1)

            def ada(j):
                src = ada_acc(j)
                if j in (4, 5):
                    pe.matmul(PS[:, 1 + j, :], ones[:, :], src, start=True, stop=False)
                    last = pe.matmul(PS[:, 1 + j, :], ones[0:1, :], brow[0:1, (j - 4) * NB:(j - 3) * NB],
                                     start=False, stop=True)
                else:
                    for q in range(4):
                        last = pe.matmul(PS[:, 7, 4 * j + q:4 * j + q + 1], src[:, q * P:(q + 1) * P],
                                         ones[:, 0:1], start=True, stop=True)
                last.then_inc(sem("ada_summed"), 1)

            def token_major(name, src, bank, per=2, rows=P, first=True, last=True, inner=NB, c0=0):
                for h in range(QUARTERS):
                    if SPLIT[quarter_no(name, h)]:
                        wait_split(pe, quarter_no(name, h))
                    else:
                        wait_loaded(pe, name, h)
                    w = slot(name, h, inner)
                    for t in range(T):
                        for o in range(inner // NB):
                            for i in range(per):
                                c = c0 + per * h + i
                                ins = product(pe, PS[:, bank(t, o), :], src[0:rows, c, t * P:(t + 1) * P],
                                              w[0:rows, i, o * NB:(o + 1) * NB],
                                              start=first and h == 0 and i == 0,
                                              stop=last and h == QUARTERS - 1 and i == per - 1)
                    free_slot(name, h, ins)

            def feature_major(name, q, width, place):
                wait_split(pe, quarter_no(name, q))
                w = slot(name, q, P)
                for c in range(KC):
                    ins = product(pe, place, w[:, c, 0:width], hT[:, c, :], start=(c == 0), stop=(c == KC - 1))
                return ins

            def attention(tag):
                units, LB, PT, asm = ATTN[tag]
                n = len(units)

                def logits(u):
                    x = units[u]
                    if u >= 2:
                        pe.wait_ge(sem(f"{tag}_max"), u - 1)
                    pe.matmul(PS[:, u % 2, 0:x["n"] * P], x["q"], x["k"], start=True,
                              stop=True).then_inc(sem(f"{tag}_logits"), 1)

                def turn(u):
                    x = units[u]
                    pe.wait_ge(sem(f"{tag}_norm"), u + 1)
                    if u >= 2:
                        pe.wait_ge(sem(f"{tag}_kept"), u - 1)
                    for j in range(x["n"]):
                        last = pe.transpose(PS[:, 2 + u % 2, j * P:(j + 1) * P], LB[:, u % 3, j * P:(j + 1) * P],
                                            ident[:, :])
                    last.then_inc(sem(f"{tag}_turned"), 1)

                def values(u):
                    x = units[u]
                    pe.wait_ge(sem(f"{tag}_kept"), u + 1)
                    for j in range(x["n"]):
                        last = pe.matmul(x["out"], x["v"][j], PT[:, u % 3, j, :], start=x["start"] and j == 0,
                                         stop=x["start"] and j == x["n"] - 1, skip_group_check=not x["start"])
                    last.then_inc(sem(f"{tag}_values"), 1)

                for u in range(n + 3):
                    if u < n:
                        logits(u)
                    if 0 <= u - 2 < n:
                        turn(u - 2)
                    if 0 <= u - 3 < n:
                        values(u - 3)

            pe.wait_ge(sem("small_loaded"), SMALL_ALL)
            for j in range(4):
                wait_used(pe, f"ada{j}")
                ada(j)
            transposes("n1", XN1, "n1_scaled", T)
            for i in range(Z1B):
                if i == 0:
                    pe.wait_ge(sem("n1_split"), 2)
                if i >= 2:
                    pe.wait_ge(sem("z_kept"), 2 * (i - 1))
                token_major(f"in{i}", hT, lambda t, o, i=i: (2 * i + t) % 4)
            pe.wait_ge(sem("later_loaded"), LATER_ALL)
            pe.wait_ge(sem("z_kept"), 2 * Z1B)
            for g in range(4):
                for t in range(T):
                    last = pe.matmul(PS[:, 2 + g // 2, (g % 2) * S:(g % 2 + 1) * S],
                                     Z[:, t, P1 + g * P:P1 + (g + 1) * P], band[:, t, g, :],
                                     start=(t == 0), stop=(t == T - 1))
            last.then_inc(sem("pool_meaned"), 1)
            pe.wait_ge(sem("pool_means_kept"), 1)
            for g in range(4):
                last = pe.matmul(PS[:, 4 + g // 2, (g % 2) * S:(g % 2 + 1) * S], wpool[:, g, :], mixT[:, g, :],
                                 start=True, stop=True)
            last.then_inc(sem("pool_mixed"), 1)
            transposes("qk1", N1, "qk1_normed", 1)
            pe.wait_ge(sem("qk1_kept"), KC)
            pe.wait_ge(sem("pool_kept"), 4)
            for t in range(T):
                for h in range(HI):
                    lo = HD * (h % 2)
                    last = pe.matmul(PS[:, 4 + 2 * t + h % 2, (h // 2) * S:(h // 2) * S + (t + 1) * P],
                                     NT1[lo:lo + HD, 5 + h // 2, t * P:(t + 1) * P],
                                     NT1[lo:lo + HD, 7, 0:(t + 1) * P], start=True, stop=True)
                last.then_inc(sem("index_products"), 1)
            pe.wait_ge(sem("chosen"), T)
            attention("a1")
            pe.wait_ge(sem("attn1_kept"), 4)
            token_major("up_attn", OT1, lambda t, o: 2 * t + o, per=1, inner=D)
            token_major("up_pool", poolT, lambda t, o: 4 + 2 * t + o, per=1, inner=D)
            pe.wait_ge(sem("m1_ready"), 1)
            for j in range(4, ADA_B):
                if j < ADA_DVE:
                    wait_used(pe, f"ada{j}")
                else:
                    pe.wait_ge(sem("pool_step"), 11 * (j - ADA_DVE + 1))
                ada(j)
            transposes("m1", M1, "m1_ready", 1)
            pe.wait_ge(sem("m1_kept"), KC)
            pe.wait_ge(sem("gate1_kept"), 2)
            pe.wait_ge(sem("ada_kept"), 2)
            for half in range(2):
                token_major(f"out{half}", MT1, lambda t, o, half=half: 4 + 2 * t + half)
            transposes("n2", XN1, "n2_scaled", T)
            pe.wait_ge(sem("n2_split"), 2)
            for i in range(2):
                for q in range(QUARTERS):
                    h = QUARTERS * i + q
                    ins = feature_major(f"pq{i}", q, P, PS[:, h // 2, (h % 2) * S:(h % 2 + 1) * S])
                    free_slot(f"pq{i}", q, ins)
            pe.wait_ge(sem("peer_q_kept"), 4)
            for t in range(T):
                for h in range(PH):
                    for p in range(2):
                        last = pe.matmul(PS[:, 4 * t + 2 * (h // 4) + p, (h % 4) * NK:(h % 4 + 1) * NK],
                                         QTP[HD * p:HD * (p + 1), h, t * P:(t + 1) * P],
                                         SK[HD * p:HD * (p + 1), h, :], start=True, stop=True)
                    if h % 4 == 3:
                        last.then_inc(sem("peer_scored"), 1)

            def peer_u(m, r=0):
                b = QUARTERS * AT["u0"] + m
                wait_split(pe, b, 2 * r)
                if m % 2 == 0:
                    pe.wait_ge(sem("u_banks_free"), m // 2 + 1 + 4 * r)
                w = parts(b)
                for c in range(KC):
                    last = product(pe, PS[:, m % 8 // 2, (m % 2) * S:(m % 2 + 1) * S], w[:, c * NK:(c + 1) * NK],
                                   hT[:, c, :], start=(c == 0), stop=(c == KC - 1))
                last.then_inc(multiplied[b % RING], 1)

            with pe.Fori(0, U_EARLY // 8) as r:
                for k in range(8):
                    peer_u(k, r)
            pe.wait_ge(sem("slots_ready"), 1)
            for w in range(3):
                for t in range(T):
                    last = pe.transpose(PS[:, 6 + w // 2, (w % 2) * S + t * P:(w % 2) * S + (t + 1) * P],
                                        SLOT[:, w, t, :], ident[:, :])
            last.then_inc(sem("slots_turned"), 1)
            with pe.Fori(U_EARLY // 8, NK // 8) as r:
                for k in range(8):
                    peer_u(k, r)

            def gates(g, r=0):
                pe.wait_ge(sem("first_rows_ready"), g + 1 + 2 * r)
                pe.wait_ge(sem("second_rows_ready"), g + 1 + 2 * r)
                pe.wait_ge(sem("gate_banks_free"), g + 1 + 2 * r)
                for j in range(4):
                    last = pe.matmul(PS[:, g % 2, j * P:(j + 1) * P], onehot[:, 0, g % 2, j, :],
                                     onehot[:, 1, g % 2, j, :], start=True, stop=True)
                last.then_inc(sem("gates_placed"), 1)

            pe.sem_inc(sem("gates_placed"), 1)
            with pe.Fori(0, S // 8) as r:
                for g in range(2):
                    gates(g, r)

            def peer_v(m, r=0, first=False):
                b = QUARTERS * AT["v0"] + m
                wait_split(pe, b, r)
                pe.wait_ge(sem("weights_split"), m + 1 + 4 * r)
                w = parts(b)
                for c in range(KC):
                    last = product(pe, PS[:, 4 + c // 2, (c % 2) * S:(c % 2 + 1) * S], w[:, c * P:(c + 1) * P],
                                   staged[:, m % 4, :], start=first and c % 2 == 0, stop=False,
                                   skip_group_check=True)
                last.then_inc(multiplied[b % RING], 1)

            for k in range(4):
                peer_v(k, first=(k == 0))
            with pe.Fori(0, NK // 4 - 1) as r:
                for k in range(4, 8):
                    peer_v(k, r)
            pe.wait_ge(sem("peer_out_kept"), KC)
            for t in range(T):
                for half in range(2):
                    for c in range(4):
                        last = pe.transpose(PS[:, 2 * t + half, c * P:(c + 1) * P],
                                            normed2[:, 4 * half + c, t * P:(t + 1) * P], ident[:, :])
                    last.then_inc(sem("peer_out_turned"), 1)

            transposes("n3", XN2, "n3_scaled", T)
            pe.wait_ge(sem("n3_split"), 2)
            for i in range(2 * RB):
                name, q = f"r{i // QUARTERS}", i % QUARTERS
                if i >= 4:
                    pe.wait_ge(sem("r_kept"), i - 3)
                ins = feature_major(name, q, RW, PS[0:RW, i % 4, 0:S])
                k = i - (2 * RB - 2)
                if k >= 0:
                    w = slot(name, q, P)
                    for t in range(T):
                        for c in range(KC):
                            ins = product(pe, PS[:, 4, t * HD + k * GATES // 2:t * HD + (k + 1) * GATES // 2],
                                          hT[:, c, t * P:(t + 1) * P], w[:, c, RW:RW + GATES // 2],
                                          start=(c == 0), stop=(c == KC - 1))
                free_slot(name, q, ins)

            def z2(i):
                if i < 2:
                    pe.wait_ge(sem("r_kept"), 2 * RB + T)
                else:
                    pe.wait_ge(sem("z2_kept"), 2 * (i - 1))
                token_major(f"z{i}", hT, lambda t, o: 4 + (2 * i + t) % 4)

            z2(0)
            z2(1)
            for q in range(QUARTERS):
                wait_loaded(pe, "rgate", q)
            w = [ring[0:RW, quarter_no("rgate", q) % RING, 0:RB // 2 * RW].rearrange("p (b n) -> p b n", b=RB // 2)
                 for q in range(QUARTERS)]
            for n in range(RB):
                pe.wait_ge(sem("conv_done"), n + 1)
                if n >= 4:
                    pe.wait_ge(sem("rgate_kept"), 2 * (n - 3))
                for k in range(2):
                    last = pe.matmul(PS[0:RW, n % 4, k * S:(k + 1) * S], w[2 * k + n // 8][:, n % 8, :],
                                     XC[0:RW, n, :], start=True, stop=True)
                    if k == 0 and n in (RB // 2 - 1, RB // 2, RB - 1):
                        free_slot("rgate", {RB // 2 - 1: 0, RB // 2: 2, RB - 1: 1}[n], last)
                if n < RB - 1:
                    last.then_inc(sem("rgate_done"), 1)
            free_slot("rgate", 3, last)
            for i in range(2, Z2B):
                z2(i)
            pe.wait_ge(sem("z2_kept"), 2 * Z2B)
            pe.wait_ge(sem("rec_out"), 1)
            transposes("q2", N2, "n2_filled", 1)
            pe.wait_ge(sem("q2_kept"), KC)
            transposes("k2", N2, "n2_filled", 2)
            pe.wait_ge(sem("k2_kept"), KC)
            transposes("c2", N2, "n2_filled", 3)
            pe.wait_ge(sem("c2_kept"), 2 * KC)
            for q in range(QUARTERS):
                kv = q // 2
                wait_loaded(pe, "cmp", q)
                w = slot("cmp", q, P)
                ls = range(q % 2 * CLEN // 4, (q % 2 + 1) * CLEN // 4)
                for l in ls:
                    pe.matmul(PS[:, kv, 0:KV * NCMP], w[:, l % (CLEN // 4), :],
                              CT2[:, KV * kv:KV * (kv + 1), 2 * l:2 * l + CSTEP * (NCMP - 1) + 1:CSTEP],
                              start=(l == 0), stop=(l == CLEN // 2 - 1))
                for l in ls:
                    last = pe.matmul(PS[:, 2 + kv, 0:1], w[:, l % (CLEN // 4), :],
                                     col("pek" if kv == 0 else "pev", l), start=(l == 0), stop=(l == CLEN // 2 - 1))
                free_slot("cmp", q, last)
            for i in range(4):
                pe.wait_ge(sem("fours_split"), i + 1)
                token_major(f"ro{i}", hT, lambda t, o: 4 + 2 * t + o, per=1, rows=RW, first=(i == 0), last=(i == 3),
                            inner=D, c0=4 * (i % 2))
            pe.wait_ge(sem("hidden_kept"), 3)
            pe.wait_ge(sem("consts2_loaded"), 16)
            pe.matmul(PS[0:HD, 0, 128:128 + HD], HID[:, 0, 0:HD], w2k, start=True, stop=True)
            pe.matmul(PS[:, 1, 128:128 + HD], HID[:, 1, :], w2v, start=True, stop=True).then_inc(sem("cmp_made"), 1)
            pe.wait_ge(sem("kcmp_normed"), 1)
            pe.transpose(PS[:, 2, 0:HD], kcmp[0:HD, 1, :], ident[0:HD, 0:HD]).then_inc(sem("kcmp_turned"), 1)
            pe.wait_ge(sem("kcmp_kept"), 1)
            for t in range(T):
                for h in range(H2):
                    lo, g = HD * (h % 2), h // (H2 // KV)
                    o = (t * H2 // 2 + h // 2) * 16
                    last = pe.matmul(PS[:, 3 * (h % 2), o:o + 16],
                                     QT2[lo:lo + HD, h // 2, t * P:(t + 1) * P],
                                     kcmp[lo:lo + HD, 2, g * 16:(g + 1) * 16], start=True, stop=True)
            last.then_inc(sem("cmp_logits"), 1)
            pe.wait_ge(sem("rec_gated"), 4)
            transposes("pz", PZ, "cmp_probs", 1)
            pe.wait_ge(sem("pz_kept"), KC)
            for h in range(H2):
                lo, hp = HD * (h % 2), h // 2
                pe.matmul(PS[lo:lo + HD, 4 + hp // 2, (hp % 2) * S:(hp % 2 + 1) * S], vcmp[lo:lo + HD, :],
                          PZT[lo:lo + HD, hp, :], start=(hp % 2 == 0), stop=False, skip_group_check=True)
            attention("a2")
            pe.wait_ge(sem("attn2_kept"), KC)
            for half in range(2):
                token_major(f"ao{half}", OT2, lambda t, o, half=half: 2 * t + half)
            transposes("m2", M2, "m2_ready", 4)
            pe.wait_ge(sem("m2_kept"), KC)
            for half in range(2):
                token_major(f"oo{half}", MT2, lambda t, o, half=half: 4 + 2 * t + half)
            transposes("n4", XN4, "n4_scaled", T)
            pe.wait_ge(sem("n4_split"), 2)
            for f in range(F_B):
                for w_, name in enumerate(("fg", "fv")):
                    if f >= 2:
                        pe.wait_ge(sem(f"{name}_read"), 4 * (f - 1))
                    for q in range(QUARTERS):
                        ins = feature_major(f"{name}{f}", q, P, PS[:, 4 * (f % 2) + 2 * w_ + q // 2,
                                                                   (q % 2) * S:(q % 2 + 1) * S])
                        free_slot(f"{name}{f}", q, ins)
            for i in range(6):
                pe.wait_ge(sem("fours_split"), 4 + i + 1)
                if i == 0:
                    pe.wait_ge(sem("fv_read"), 4 * (F_B - 1))
                token_major(f"dn{i}", hT, lambda t, o: 2 * t + o, per=1, first=(i == 0), last=(i == 5), inner=D,
                            c0=4 * (i % 2))

        @block.scalar
        def _(act):
            steps = [0]

            def link(ins):
                steps[0] += 1
                ins.then_inc(sem("act_step"), 1)
                act.wait_ge(sem("act_step"), steps[0])

            rounding = [0]

            def round_quarter(b, r=0):
                act.wait_ge(loaded[b % RING], 16 * (b // RING + 1) + 16 * r)
                if nth_split(b) > 1:
                    act.wait_ge(multiplied[b % RING], nth_split(b) - 1 + r)
                act.activation(high[:, b % RING, :], ring[:, b % RING, :],
                               ACT.Copy).then_inc(rounded[b % RING], 1)

            def ahead(name, q=QUARTERS - 1, n=RING - 1):
                while rounding[0] <= min(quarter_no(name, q) + n, N_QUARTERS - 1):
                    if SPLIT[rounding[0]]:
                        round_quarter(rounding[0])
                    rounding[0] += 1

            def wait_product(name, q=QUARTERS - 1):
                ahead(name, q)
                wait_used(act, name, q)

            def sumsq(tag, XN, ready=None, n=0):
                if ready:
                    act.wait_ge(sem(ready), n)
                for t in range(T):
                    act.activation(XN[:, t, :], X[:, t, :], ACT.Square,
                                   accum_out=tiny[:, t:t + 1]).then_inc(sem(f"{tag}_sumsq"), 1)
                act.wait_ge(sem(f"{tag}_meansq"), 1)
                act.activation(tiny[:, 4:4 + T], tiny[:, 2:2 + T], ACT.Sqrt).then_inc(sem(f"{tag}_root"), 1)

            def keep_turned(tag, dst, scale=None, shift=None):
                for c in range(KC // 2):
                    act.wait_ge(sem(f"{tag}_turned"), c // 2 + 1)
                    kw = {}
                    if scale:
                        kw["scale"] = scale(c)
                    if shift:
                        kw["bias"] = shift(c)
                    act.activation(dst[:, c, :], PS[:, c // 2, (c % 2) * S:(c % 2 + 1) * S],
                                   ACT.Identity if kw else ACT.Copy, **kw).then_inc(sem(f"{tag}_kept"), 1)

            def attention(tag, scale):
                units, LB, PT, asm = ATTN[tag]
                n = len(units)

                def kept(u):
                    x = units[u]
                    act.wait_ge(sem(f"{tag}_turned"), u + 1)
                    if u >= 3:
                        act.wait_ge(sem(f"{tag}_values"), u - 2)
                    act.activation(PT[:, u % 3, 0:x["n"], :].rearrange("p j q -> p (j q)"),
                                   PS[:, 2 + u % 2, 0:x["n"] * P], ACT.Copy).then_inc(sem(f"{tag}_kept"), 1)

                for u in range(n + 2):
                    if u < n:
                        x = units[u]
                        act.wait_ge(sem(f"{tag}_negmax"), u + 1)
                        act.activation(LB[:, u % 3, 0:x["n"] * P], LB[:, u % 3, 0:x["n"] * P], ACT.Exp, scale=scale,
                                       bias=asm[:, 1, u % 3:u % 3 + 1],
                                       accum_out=asm[:, 2, u % 3:u % 3 + 1]).then_inc(sem(f"{tag}_exp"), 1)
                    if 0 <= u - 2 < n:
                        kept(u - 2)

            act.wait_ge(sem("small_loaded"), SMALL_ALL)
            sumsq("n1", XN1)
            act.wait_ge(sem("ada_kept"), 1)
            later = sem("later_loaded")
            act.dma_start(band, a["band"].rearrange("p (t g s) -> p t g s", t=T, g=4)).then_inc(later, 16)
            act.dma_start(wpool, a["wpool"].rearrange("p (g d) -> p g d", g=4)).then_inc(later, 16)
            act.dma_start(brow[0:1, :], a["brow"]).then_inc(later, 16)
            act.dma_start(SK, a["skeys"].rearrange("p (h k) -> p h k", h=PH)).then_inc(later, 16)
            act.dma_start(iota[:, :], a["consts"][:, P:2 * P]).then_inc(later, 16)
            keep_turned("n1", normed1, lambda c: adaT[:, 8 + c:9 + c], lambda c: adaT[:, c:c + 1])
            for i in range(Z1B):
                wait_product(f"in{i}")
                for t in range(T):
                    act.activation(Z[:, t, i * NB:(i + 1) * NB], PS[:, (2 * i + t) % 4, :],
                                   ACT.Copy).then_inc(sem("z_kept"), 1)
            act.wait_ge(sem("qk1_meansq"), 1)
            act.activation(st1[:, 1, :], st1[:, 0, :], ACT.Sqrt).then_inc(sem("qk1_root"), 1)
            act.wait_ge(sem("pool_meaned"), 1)
            act.activation(mixT.rearrange("p g s -> p (g s)"), PS[:, 2:4, :].rearrange("p b n -> p (b n)"),
                           ACT.Copy).then_inc(sem("pool_means_kept"), 1)
            act.wait_ge(sem("pool_mixed"), 1)
            for g in range(4):
                act.activation(poolT[:, g, :], PS[:, 4 + g // 2, (g % 2) * S:(g % 2 + 1) * S], ACT.Copy,
                               scale=col("spool", g)).then_inc(sem("pool_kept"), 1)
            keep_turned("qk1", NT1, lambda c: col("gain1", c))
            act.wait_ge(sem("z_kept"), 2 * Z1B)
            for t in range(T):
                act.activation(Z[:, t, G1:G1 + 2 * D], Z[:, t, G1:G1 + 2 * D],
                               ACT.Sigmoid).then_inc(sem("sig1"), 1)
            attention("a1", HD ** -0.5)
            act.wait_ge(sem("a1_values"), len(ATTN["a1"][0]))
            for c in range(4):
                act.activation(OT1[:, c, :], PS[:, 4 + c // 2, (c % 2) * S:(c % 2 + 1) * S],
                               ACT.Copy).then_inc(sem("attn1_kept"), 1)
            for i in range(2):
                act.wait_ge(sem("ada_summed"), 5 + i)
                act.activation(gate1[:, i * NB:(i + 1) * NB], PS[:, 5 + i, :],
                               ACT.Copy).then_inc(sem("gate1_kept"), 1)
            keep_turned("m1", MT1)
            ahead("out1")
            sumsq("n2", XN1, "x1_ready", 4)
            keep_turned("n2", normed1, lambda c: adaT[:, 32 + c:33 + c], lambda c: adaT[:, 24 + c:25 + c])
            for i in range(2):
                for j in range(2):
                    wait_product(f"pq{i}", 2 * j + 1)
                    act.activation(QTP[:, 4 * i + 2 * j:4 * i + 2 * j + 2, :].rearrange("p c s -> p (c s)"),
                                   PS[:, 2 * i + j, :], ACT.Copy).then_inc(sem("peer_q_kept"), 1)
            for i in range(8):
                t, q, p = i // 4, i // 2 % 2, i % 2
                act.wait_ge(sem("peer_scored"), i // 2 + 1)
                act.activation(SX[:, t, :, :].rearrange("p (h w) n -> p w h n", w=2)[:, p, 4 * q:4 * q + 4, :],
                               PS[:, i, :].rearrange("p (h n) -> p h n", h=4),
                               ACT.Copy).then_inc(sem("scores_kept"), 1)
            act.wait_ge(sem("scores_kept"), 8)
            act.sem_inc(sem("u_banks_free"), 4)

            def gelu_u(m, r=0):
                b = QUARTERS * AT["u0"] + m
                round_quarter(b + 3, 2 * r)
                round_quarter(b + 4, 2 * r)
                act.wait_ge(multiplied[(b + 1) % RING], nth_split(b + 1) + 2 * r)
                act.activation(region[:, bass.ds(m * S + r * (8 * S), 2 * S)], PS[:, m % 8 // 2, :],
                               ACT.Gelu).then_inc(sem("u_banks_free"), 1)

            ahead("u0", 0, 2)
            with act.Fori(0, U_EARLY // 8) as r:
                for k in range(0, 8, 2):
                    gelu_u(k, r)
            act.dma_start(out.rearrange("(t p) d -> p t d", p=P), X[:, :, :]).then_inc(sem("x_moved"), 16)
            act.wait_ge(sem("best_less_max"), 1)
            act.activation(BE.rearrange("p t h k -> p (t h k)"), BE.rearrange("p t h k -> p (t h k)"),
                           ACT.Exp).then_inc(sem("best_exp"), 1)
            act.wait_ge(sem("slots_saved"), 3)
            with act.Fori(U_EARLY // 8, NK // 8) as r:
                for k in range(0, 8, 2):
                    gelu_u(k, r)
            def first_rows(g, r=0):
                if not (isinstance(r, int) and g < 2):
                    act.wait_ge(sem("gates_placed"), g + 2 * r)
                for j in range(4):
                    act.activation(onehot[:, 0, g % 2, j, :], iota[:, :], ACT.Square,
                                   bias=slotT[:, 0, bass.ds(4 * g + j + 8 * r, 1)]).then_inc(sem("rows_squared"), 1)
                act.wait_ge(sem("rows_squared"), 4 * (g + 1) + 8 * r)
                rows = onehot[:, 0, g % 2, :, :].rearrange("p j k -> p (j k)")
                act.activation(rows, rows, ACT.Relu, scale=-1.0,
                               bias=ones[:, 0:1]).then_inc(sem("first_rows_ready"), 1)

            act.wait_ge(sem("x_moved"), 16)
            first_rows(0)
            with act.Fori(0, S // 8 - 1) as r:
                first_rows(1, r)
                first_rows(2, r)
            first_rows(S // 4 - 1)
            with act.Fori(0, NK // 4 - 1) as r:
                for k in range(3, 7):
                    round_quarter(QUARTERS * AT["v0"] + k, r)
            round_quarter(QUARTERS * AT["v0"] + NK - 1)
            rounding[0] = QUARTERS * AT["v0"] + NK
            act.wait_ge(sem("gate_banks_free"), 2 + S // 4)
            act.dma_start(X[:, :, :], out.rearrange("(t p) d -> p t d", p=P)).then_inc(sem("x_moved"), 16)
            wait_used(act, f"v{U_BLOCKS - 1}")
            act.dma_start(C2, a["consts2"]).then_inc(sem("consts2_loaded"), 16)
            for c in range(KC // 2):
                act.activation(normed2[:, c, :], PS[:, 4 + c // 2, (c % 2) * S:(c % 2 + 1) * S], ACT.Copy,
                               scale=adaT[:, 40 + c:41 + c]).then_inc(sem("peer_out_kept"), 1)

            sumsq("n3", XN2, "x2_ready", 4)
            keep_turned("n3", normed2, lambda c: col("n1", c))
            act.wait_ge(sem("lam_abs"), 1)
            act.activation(sp[0:RW, 1, :], sp[0:RW, 0, :], ACT.Exp, scale=-1.0).then_inc(sem("lam_exp"), 1)
            for i in range(2 * RB):
                wait_product(f"r{i // QUARTERS}", i % QUARTERS)
                act.activation(RX[0:RW, i, :] if i < RB else RGT[0:RW, i - RB, :], PS[0:RW, i % 4, 0:S],
                               ACT.Copy if i < RB else ACT.Gelu_apprx_tanh).then_inc(sem("r_kept"), 1)
            for t in range(T):
                act.activation(NSG[:, t, :], PS[:, 4, t * HD:t * HD + GATES], ACT.Sigmoid).then_inc(sem("r_kept"), 1)

            def z2(i):
                wait_product(f"z{i}")
                for t in range(T):
                    act.activation(Z2[:, t, i * NB:(i + 1) * NB], PS[:, 4 + (2 * i + t) % 4, :],
                                   ACT.Copy).then_inc(sem("z2_kept"), 1)

            z2(0)
            z2(1)
            act.wait_ge(sem("decay_ready"), 1)
            for n in range(RB):
                if n < RB - 1:
                    act.wait_ge(sem("rgate_done"), n + 1)
                else:
                    wait_product("rgate")
                act.activation(RT[0:RW, n, :], PS[0:RW, n % 4, 0:S], ACT.Sigmoid,
                               bias=col("ba", n, RW)).then_inc(sem("rgate_kept"), 1)
                act.activation(IT[0:RW, n, :], PS[0:RW, n % 4, S:2 * S], ACT.Sigmoid,
                               bias=col("bx", n, RW)).then_inc(sem("rgate_kept"), 1)
            for n in range(RB):
                act.wait_ge(sem("rgate_kept"), 2 * n + 2)
                act.activation(RT[0:RW, n, :], RT[0:RW, n, :], ACT.Tanh,
                               scale=sp[0:RW, 7, n:n + 1]).then_inc(sem("tanh_done"), 1)
            act.wait_ge(sem("tanh_done"), RB)
            act.wait_ge(sem("xc_used"), 1)
            act.activation(XC[0:RW, :, :].rearrange("p b s -> p (b s)"),
                           RT[0:RW, :, :].rearrange("p b s -> p (b s)"), ACT.Sqrt).then_inc(sem("root_tanh"), 1)
            for i in range(2, Z2B):
                z2(i)
            act.wait_ge(sem("z2_kept"), 2 * Z2B)
            act.wait_ge(sem("rec_out"), 1)
            for t in range(T):
                act.activation(SQ2[:, t, 0:1024], Z2[:, t, 0:1024], ACT.Square).then_inc(sem("sq2"), 1)
                act.activation(SQ2[:, t, 1024:1280], Z2[:, t, KS2:KS2 + 256], ACT.Square).then_inc(sem("sq2"), 1)
                act.activation(SQ2[:, t, 1280:1536], Z2[:, t, KW2:KW2 + 256], ACT.Square).then_inc(sem("sq2"), 1)
            act.wait_ge(sem("qk2_meansq"), 1)
            act.activation(st2[:, 1, :], st2[:, 0, :], ACT.Sqrt).then_inc(sem("qk2_root"), 1)
            keep_turned("q2", QT2, lambda c: col("gainq"))
            keep_turned("k2", KT2, lambda c: col("gainks"))
            for c in range(KC // 2):
                act.wait_ge(sem("c2_turned"), c // 2 + 1)
                src = PS[:, c // 2, (c % 2) * S:(c % 2 + 1) * S]
                act.activation(CT2[0:HD, c, :], src[0:HD, :], ACT.Copy).then_inc(sem("c2_kept"), 1)
                act.activation(CT2[HD:P, c, 0:S - 1], src[HD:P, 1:S], ACT.Copy).then_inc(sem("c2_kept"), 1)
            for t in range(T):
                act.activation(Z2[:, t, MR2:MR2 + 2 * D], Z2[:, t, MR2:MR2 + 2 * D],
                               ACT.Sigmoid).then_inc(sem("sig2"), 1)
            wait_product("cmp")
            act.wait_ge(sem("pe_bias"), 1)
            hk = HID[:, 0, 0:HD].rearrange("p (g i) -> p g i", g=KV)[:, :, 0:NCMP]
            act.activation(hk, PS[:, 0, 0:KV * NCMP].rearrange("p (g i) -> p g i", g=KV), ACT.Gelu_apprx_tanh,
                           bias=PEB[:, 0:1]).then_inc(sem("hidden_kept"), 1)
            for dup in range(2):
                hv = HID[:, 1, dup * HD:(dup + 1) * HD].rearrange("p (g i) -> p g i", g=KV)[:, :, 0:NCMP]
                act.activation(hv, PS[:, 1, 0:KV * NCMP].rearrange("p (g i) -> p g i", g=KV), ACT.Gelu_apprx_tanh,
                               bias=PEB[:, 1:2]).then_inc(sem("hidden_kept"), 1)
            ahead("ro3", n=0)
            act.wait_ge(sem("kcmp_meansq"), 1)
            act.activation(cst[0:HD, 1, 0:1], cst[0:HD, 0, 0:1], ACT.Sqrt).then_inc(sem("kcmp_root"), 1)
            act.wait_ge(sem("cmp_less_max"), 1)
            act.activation(LC.rearrange("p t s -> p (t s)"), LC.rearrange("p t s -> p (t s)"),
                           ACT.Exp).then_inc(sem("cmp_exp"), 1)
            keep_turned("pz", PZT)
            attention("a2", HD ** -0.5)
            act.wait_ge(sem("a2_values"), len(ATTN["a2"][0]))
            for c in range(KC):
                act.activation(OT2[:, c, :], PS[:, 4 + c // 2, (c % 2) * S:(c % 2 + 1) * S],
                               ACT.Copy).then_inc(sem("attn2_kept"), 1)
            keep_turned("m2", MT2)
            sumsq("n4", XN4, "x3_ready", 4)
            ahead("fg0", 0)
            keep_turned("n4", normed2, lambda c: col("n2", c))
            for f in range(F_B):
                for q in range(4):
                    ahead(f"fg{f}", q)
                    act.wait_ge(sem("fg_conv"), 4 * f + q + 1)
                    act.activation(CG[:, q, :], CG[:, q, :], ACT.Gelu_apprx_tanh).then_inc(sem("fg_gelu"), 1)
            ahead("dn5")

        @block.vector
        def _(dve):
            steps = [0]

            def link(ins):
                steps[0] += 1
                ins.then_inc(sem("dve_step"), 1)
                dve.wait_ge(sem("dve_step"), steps[0])

            def scaled(tag, XN):
                dve.wait_ge(sem(f"{tag}_sumsq"), T)
                dve.tensor_scalar(tiny[:, 2:2 + T], tiny[:, 0:T], 1.0 / D, EPS, ALU.mult,
                                  ALU.add).then_inc(sem(f"{tag}_meansq"), 1)
                dve.wait_ge(sem(f"{tag}_root"), 1)
                link(dve.reciprocal(tiny[:, 6:6 + T], tiny[:, 4:4 + T]))
                for t in range(T):
                    dve.tensor_scalar(XN[:, t, :], X[:, t, :], tiny[:, 6 + t:7 + t], None,
                                      ALU.mult).then_inc(sem(f"{tag}_scaled"), 1)

            def split_input(tag, src):
                for i, c in enumerate((slice(0, KC // 2), slice(KC // 2, KC))):
                    dve.wait_ge(sem(f"{tag}_kept"), KC)
                    link(dve.tensor_copy(hTh[:, c, :], src[:, c, :]))
                    dve.tensor_tensor(hTl[:, c, :], src[:, c, :], hTh[:, c, :].bitcast(F32),
                                      ALU.subtract).then_inc(sem(f"{tag}_split"), 1)

            def split_fours(name, src, i, before, rows=P):
                wait_used(dve, f"{name}{i - 2}" if i >= 2 else before)
                half, c = slice(4 * (i % 2), 4 * (i % 2) + 4), slice(4 * i, 4 * i + 4)
                link(dve.tensor_copy(hTh[0:rows, half, :], src[0:rows, c, :]))
                dve.tensor_tensor(hTl[0:rows, half, :], src[0:rows, c, :], hTh[0:rows, half, :].bitcast(F32),
                                  ALU.subtract).then_inc(sem("fours_split"), 1)

            def keep_turned(tag, dst, scale=None, shift=None):
                for c in range(KC // 2, KC):
                    dve.wait_ge(sem(f"{tag}_turned"), c // 2 + 1)
                    src = PS[:, c // 2, (c % 2) * S:(c % 2 + 1) * S]
                    if scale and shift:
                        ins = dve.tensor_scalar(dst[:, c, :], src, scale(c), shift(c), ALU.mult, ALU.add)
                    elif scale:
                        ins = dve.tensor_scalar(dst[:, c, :], src, scale(c), None, ALU.mult)
                    else:
                        ins = dve.tensor_copy(dst[:, c, :], src)
                    ins.then_inc(sem(f"{tag}_kept"), 1)

            def attention(tag, scale):
                units, LB, PT, asm = ATTN[tag]
                n = len(units)
                for u in range(n + 1):
                    if u < n:
                        x = units[u]
                        dve.wait_ge(sem(f"{tag}_logits"), u + 1)
                        if u >= 3:
                            dve.wait_ge(sem(f"{tag}_turned"), u - 2)
                        dve.tensor_tensor_reduce(LB[:, u % 3, 0:x["n"] * P], PS[:, u % 2, 0:x["n"] * P], x["mask"],
                                                 1.0, TAKEN, ALU.add, ALU.max,
                                                 asm[:, 0, u % 3:u % 3 + 1]).then_inc(sem(f"{tag}_max"), 1)
                        dve.wait_ge(sem(f"{tag}_max"), u + 1)
                        dve.tensor_scalar(asm[:, 1, u % 3:u % 3 + 1], asm[:, 0, u % 3:u % 3 + 1], -scale, None,
                                          ALU.mult).then_inc(sem(f"{tag}_negmax"), 1)
                    if u >= 1:
                        v, x = (u - 1) % 3, units[u - 1]
                        dve.wait_ge(sem(f"{tag}_exp"), u)
                        link(dve.reciprocal(asm[:, 3, v:v + 1], asm[:, 2, v:v + 1]))
                        if x["gate"] is None:
                            ins = dve.tensor_scalar(LB[:, v, 0:x["n"] * P], LB[:, v, 0:x["n"] * P],
                                                    asm[:, 3, v:v + 1], None, ALU.mult)
                        else:
                            ins = dve.tensor_scalar(LB[:, v, 0:x["n"] * P], LB[:, v, 0:x["n"] * P],
                                                    asm[:, 3, v:v + 1], x["gate"], ALU.mult, ALU.mult)
                        ins.then_inc(sem(f"{tag}_norm"), 1)

            def bc(ap, axis, n):
                v = ap.unsqueeze(axis)
                shape = list(v.shape)
                shape[axis] = n
                return v.broadcast_to(shape)

            def ada(j):
                if j in (2, 3):
                    dve.wait_ge(sem("ada_summed"), j - 1)
                for q in range(QUARTERS):
                    wait_loaded(dve, f"ada{j}", q)
                    w = slot(f"ada{j}", q)
                    if q:
                        wait_used(dve, f"ada{j}", q - 1)
                    for c in range(2):
                        if q == c == 0:
                            ins = dve.tensor_scalar(ada_acc(j), w[:, 0, :], col("cT", 0), None, ALU.mult)
                        else:
                            ins = dve.scalar_tensor_tensor(ada_acc(j), w[:, c, :], col("cT", 2 * q + c),
                                                           ada_acc(j), ALU.mult, ALU.add)
                        if c == 0:
                            link(ins)
                    free_slot(f"ada{j}", q, ins)

            dve.wait_ge(sem("small_loaded"), SMALL_ALL)
            scaled("n1", XN1)
            for j in range(4):
                ada(j)
            dve.wait_ge(sem("ada_summed"), 4)
            link(dve.tensor_tensor(adaT[:, 0:16], PS[:, 7, 0:16], cols[:, COL["bada"][0]:COL["bada"][0] + 16], ALU.add))
            dve.scalar_tensor_tensor(adaT[:, 8:16], adaT[:, 8:16], 1.0, cols[:, COL["g1"][0]:COL["g1"][0] + 8],
                                     ALU.add, ALU.mult).then_inc(sem("ada_kept"), 1)
            dve.wait_ge(sem("ada_kept"), 1)
            keep_turned("n1", normed1, lambda c: adaT[:, 8 + c:9 + c], lambda c: adaT[:, c:c + 1])
            split_input("n1", normed1)
            for j in range(4, ADA_DVE):
                ada(j)
            dve.wait_ge(sem("z_kept"), 2 * Z1B)
            for t in range(T):
                link(dve.tensor_tensor(sq1[:, t, 0:576], Z[:, t, 0:576], Z[:, t, 0:576], ALU.mult))
                link(dve.tensor_tensor(sq1[:, t, 576:640], Z[:, t, IK1:IK1 + HD], Z[:, t, IK1:IK1 + HD], ALU.mult))
            link(dve.tensor_reduce(st1[:, 2, :], sq1.rearrange("p t (h d) -> p (t h) d", d=HD), AX_X, ALU.add))
            dve.tensor_scalar(st1[:, 0, :], st1[:, 2, :], 1.0 / HD, EPS, ALU.mult, ALU.add).then_inc(sem("qk1_meansq"), 1)
            dve.wait_ge(sem("qk1_root"), 1)
            link(dve.reciprocal(st1[:, 2, :], st1[:, 1, :]))
            for t in range(T):
                r0 = 10 * t
                dve.tensor_tensor(N1[:, t, 0:512].rearrange("p (h d) -> p h d", d=HD),
                                  Z[:, t, 0:512].rearrange("p (h d) -> p h d", d=HD),
                                  bc(st1[:, 2, r0:r0 + 8], 2, HD), ALU.mult)
                for dup in range(2):
                    dve.tensor_scalar(N1[:, t, 512 + dup * HD:576 + dup * HD], Z[:, t, K1:K1 + HD],
                                      st1[:, 2, r0 + 8:r0 + 9], None, ALU.mult)
                    dve.tensor_scalar(N1[:, t, 896 + dup * HD:960 + dup * HD], Z[:, t, IK1:IK1 + HD],
                                      st1[:, 2, r0 + 9:r0 + 10], None, ALU.mult)
                link(dve.tensor_copy(N1[:, t, 640:896], Z[:, t, IQ1:IQ1 + 256]))
            dve.memset(m8[:, :], 0.0).then_inc(sem("qk1_normed"), 1)
            keep_turned("qk1", NT1, lambda c: col("gain1", c))
            for t in range(T):
                n = (t + 1) * P
                dve.wait_ge(sem("index_products"), t + 1)
                for h in range(HI):
                    src = PS[:, 4 + 2 * t + h % 2, (h // 2) * S:(h // 2) * S + n]
                    dst = score[:, t, 0:n] if h == 0 else stmp[:, 0:n]
                    link(dve.tensor_scalar(dst, src, 0.0, Z[:, t, IW1 + h:IW1 + h + 1], ALU.max, ALU.mult))
                    if h:
                        link(dve.tensor_tensor(score[:, t, 0:n], score[:, t, 0:n], stmp[:, 0:n], ALU.add))
                link(dve.memset(score[0:HD, t, n - HD:n], BARRED))
                src = score
                for _ in range(NSEL // 8):
                    link(dve.max(m8[:, :], src[:, t, 0:n]))
                    link(dve.match_replace(work[:, t, 0:n], m8[:, :], src[:, t, 0:n], TAKEN))
                    src = work
                dve.tensor_scalar(bias1[:, t, 0:n], work[:, t, 0:n], BARRED * 2, MASKED, ALU.is_gt,
                                  ALU.mult).then_inc(sem("chosen"), 1)
            dve.wait_ge(sem("chosen"), T)
            attention("a1", HD ** -0.5)
            dve.wait_ge(sem("sig1"), T)
            wait_used(dve, "up_attn")
            wait_used(dve, "up_pool")
            for t in range(T):
                for half in range(2):
                    o = half * NB
                    link(dve.tensor_tensor(mtmp[:, 0, :], PS[:, 2 * t + half, :], Z[:, t, G1 + o:G1 + o + NB], ALU.mult))
                    link(dve.tensor_tensor(mtmp[:, 1, :], PS[:, 4 + 2 * t + half, :],
                                           Z[:, t, G1 + D + o:G1 + D + o + NB], ALU.mult))
                    link(dve.tensor_tensor(M1[:, t, o:o + NB], mtmp[:, 0, :], mtmp[:, 1, :], ALU.add))
            dve.memset(m8[:, :], 0.0).then_inc(sem("m1_ready"), 1)
            dve.wait_ge(sem("ada_summed"), ADA_B)
            dve.tensor_tensor(adaT[:, 24:48], PS[:, 7, 24:48],
                              cols[:, COL["bada"][0] + 24:COL["bada"][0] + 48], ALU.add).then_inc(sem("ada_kept"), 1)
            dve.wait_ge(sem("ada_kept"), 2)
            dve.scalar_tensor_tensor(adaT[:, 32:40], adaT[:, 32:40], 1.0, cols[:, COL["g2"][0]:COL["g2"][0] + 8],
                                     ALU.add, ALU.mult).then_inc(sem("ada_kept"), 1)
            dve.wait_ge(sem("ada_kept"), 3)
            keep_turned("m1", MT1)
            dve.wait_ge(sem("gate1_kept"), 2)
            for half in range(2):
                wait_used(dve, f"out{half}")
                for t in range(T):
                    o = half * NB
                    link(dve.tensor_tensor(mtmp[:, t, :], PS[:, 4 + 2 * t + half, :], gate1[:, o:o + NB], ALU.mult))
                    dve.tensor_tensor(X[:, t, o:o + NB], X[:, t, o:o + NB], mtmp[:, t, :],
                                      ALU.add).then_inc(sem("x1_ready"), 1)
            dve.wait_ge(sem("x1_ready"), 4)
            scaled("n2", XN1)
            keep_turned("n2", normed1, lambda c: adaT[:, 32 + c:33 + c], lambda c: adaT[:, 24 + c:25 + c])
            split_input("n2", normed1)
            for t in range(T):
                dve.wait_ge(sem("scores_kept"), 4 * (t + 1))
                for k in range(2 * PH):
                    for rnd in range(2):
                        tv = TV[:, t, k, 8 * rnd:8 * rnd + 8]
                        link(dve.max(tv, SX[:, t, k, :]))
                        link(dve.max_index(TI[:, t, k, 8 * rnd:8 * rnd + 8].bitcast(U32), tv, SX[:, t, k, :]))
                        if rnd == 0:
                            link(dve.match_replace(SX[:, t, k, :], tv, SX[:, t, k, :], TAKEN))
            for t in range(T):
                halves = TV[:, t, :, :].rearrange("p (h w) k -> p w h k", w=2)
                link(dve.tensor_tensor(CAND.rearrange("p h (x y) -> p h x y", x=TOPK),
                                       bc(halves[:, 0], 3, TOPK), bc(halves[:, 1], 2, TOPK), ALU.add))
                for h in range(PH):
                    for rnd in range(2):
                        bv = BV[:, t, h, 8 * rnd:8 * rnd + 8]
                        link(dve.max(bv, CAND[:, h, :]))
                        link(dve.max_index(BI[:, t, h, 8 * rnd:8 * rnd + 8].bitcast(U32), bv, CAND[:, h, :]))
                        if rnd == 0:
                            link(dve.match_replace(CAND[:, h, :], bv, CAND[:, h, :], TAKEN))
            dve.tensor_tensor(BE, BV, BV[:, :, :, 0:1].broadcast_to([P, T, PH, TOPK]),
                              ALU.subtract).then_inc(sem("best_less_max"), 1)
            link(dve.tensor_copy(TI, TI.bitcast(U32)))
            for t in range(T):
                bi = BI[:, t, :, :].bitcast(U32)
                for w in range(2):
                    ab = AB[:, w, :, :].bitcast(U32)
                    if w == 0:
                        link(dve.tensor_scalar(ab, bi, 4, None, ALU.logical_shift_right))
                    else:
                        link(dve.tensor_scalar(ab, bi, TOPK - 1, None, ALU.bitwise_and))
                    link(dve.tensor_copy(AB[:, w, :, :], ab))
                    keys = TI[:, t, :, :].rearrange("p (h w) k -> p w h k", w=2)[:, w]
                    link(dve.tensor_tensor(EQ, bc(AB[:, w, :, :], 3, TOPK),
                                           bc(bc(iota[:, 0:TOPK], 1, TOPK), 1, PH), ALU.is_equal))
                    link(dve.tensor_tensor(EQ, EQ, bc(keys, 2, TOPK), ALU.mult))
                    link(dve.tensor_reduce(SLOT[:, w, t, :].rearrange("p (h k) -> p h k", h=PH), EQ, AX_X, ALU.add))
            dve.wait_ge(sem("best_exp"), 1)
            link(dve.tensor_reduce(gsum[:, 0, :], BE.rearrange("p t h k -> p (t h) k"), AX_X, ALU.add))
            link(dve.reciprocal(gsum[:, 1, :], gsum[:, 0, :]))
            dve.tensor_tensor(SLOT[:, 2, :, :].rearrange("p t (h k) -> p (t h) k", h=PH),
                              BE.rearrange("p t h k -> p (t h) k"), bc(gsum[:, 1, :], 2, TOPK),
                              ALU.mult).then_inc(sem("slots_ready"), 1)
            dve.wait_ge(sem("slots_turned"), 1)
            for w in range(3):
                dve.tensor_scalar(slotT[:, w, :], PS[:, 6 + w // 2, (w % 2) * S:(w % 2 + 1) * S],
                                  -1.0 if w == 0 else 1.0, None, ALU.mult).then_inc(sem("slots_saved"), 1)
            dve.wait_ge(sem("slots_saved"), 3)
            dve.sem_inc(sem("gate_banks_free"), 2)

            def rows(g, r=0):
                if not (isinstance(r, int) and g < 2):
                    dve.wait_ge(sem("gates_placed"), g + 2 * r)
                for j in range(4):
                    n = bass.ds(4 * g + j + 8 * r, 1)
                    last = dve.tensor_scalar(onehot[:, 1, g % 2, j, :], iota[:, :], slotT[:, 1, n], slotT[:, 2, n],
                                             ALU.is_equal, ALU.mult)
                last.then_inc(sem("second_rows_ready"), 1)

            act_v = region[:, :].rearrange("p (i n) -> p i n", n=S)

            def weigh(g, r=0):
                dve.wait_ge(sem("gates_placed"), g + 2 + 2 * r)
                v = act_v[:, :, bass.ds(4 * g + 8 * r, 4)]
                dve.tensor_tensor(v, v, PS[:, g % 2, :].rearrange("p (n i) -> p i n", n=4),
                                  ALU.mult).then_inc(sem("gate_banks_free"), 1)

            dve.wait_ge(sem("u_banks_free"), 4 + NK // 2)
            dve.wait_ge(sem("x_moved"), 16)
            rows(0)
            with dve.Fori(0, S // 8 - 1) as r:
                rows(1, r)
                weigh(0, r)
                rows(2, r)
                weigh(1, r)
            rows(S // 4 - 1)
            weigh(S // 4 - 2)
            weigh(S // 4 - 1)
            dve.wait_ge(sem("gate_banks_free"), 2 + S // 4)

            def split_weights(m, r=0):
                b = QUARTERS * AT["v0"] + m
                if m >= 4:
                    dve.wait_ge(multiplied[b % RING], nth_split(b) - 1 + r)
                src = region[:, bass.ds(m * S + r * (4 * S), S)]
                hi, lo = tuple(staged[:, m % 4, :])
                dve.tensor_copy(hi, src).then_inc(sem("weights_rounded"), 1)
                dve.wait_ge(sem("weights_rounded"), m + 1 + 4 * r)
                dve.tensor_tensor(lo, src, hi.bitcast(F32), ALU.subtract).then_inc(sem("weights_split"), 1)

            for m in range(4):
                split_weights(m)
            with dve.Fori(0, NK // 4 - 1) as r:
                for k in range(4, 8):
                    split_weights(k, r)
            wait_used(dve, f"v{U_BLOCKS - 1}")
            for c in range(KC // 2, KC):
                dve.tensor_scalar(normed2[:, c, :], PS[:, 4 + c // 2, (c % 2) * S:(c % 2 + 1) * S], adaT[:, 40 + c:41 + c],
                                  None, ALU.mult).then_inc(sem("peer_out_kept"), 1)
            dve.wait_ge(sem("x_moved"), 32)
            for t in range(T):
                for half in range(2):
                    dve.wait_ge(sem("peer_out_turned"), 2 * t + half + 1)
                    xs = X[:, t, half * NB:(half + 1) * NB]
                    dve.tensor_tensor(xs, xs, PS[:, 2 * t + half, :], ALU.add).then_inc(sem("x2_ready"), 1)

            dve.wait_ge(sem("x2_ready"), 4)
            scaled("n3", XN2)
            lam = cols[0:RW, COL["lam"][0]:COL["lam"][0] + RB]
            s = [sp[0:RW, i, :] for i in range(8)]
            link(dve.tensor_scalar(s[2], lam, -1.0, None, ALU.mult))
            dve.tensor_tensor(s[0], lam, s[2], ALU.max).then_inc(sem("lam_abs"), 1)
            dve.wait_ge(sem("lam_exp"), 1)
            link(dve.tensor_scalar(s[3], s[1], 2.0, None, ALU.add))
            link(dve.reciprocal(s[4], s[3]))
            link(dve.tensor_tensor(s[5], s[1], s[4], ALU.mult))
            link(dve.tensor_tensor(s[6], s[5], s[5], ALU.mult))
            link(dve.tensor_scalar(s[7], s[6], 1.0 / 15, 1.0 / 13, ALU.mult, ALU.add))
            for k in (11, 9, 7, 5, 3, 1):
                link(dve.tensor_tensor(s[7], s[7], s[6], ALU.mult))
                link(dve.tensor_scalar(s[7], s[7], 1.0 / k, None, ALU.add))
            link(dve.tensor_tensor(s[7], s[7], s[5], ALU.mult))
            link(dve.tensor_scalar(s[7], s[7], 8.0, None, ALU.mult))
            link(dve.tensor_scalar(s[2], s[2], 0.0, 4.0, ALU.max, ALU.mult))
            dve.tensor_tensor(s[7], s[7], s[2], ALU.add).then_inc(sem("decay_ready"), 1)
            keep_turned("n3", normed2, lambda c: col("n1", c))
            split_input("n3", normed2)
            for n in range(RB):
                dve.wait_ge(sem("r_kept"), n + 1)
                link(dve.tensor_scalar(XC[0:RW, n, :], RX[0:RW, n, :], col("cw", 3 * RB + n, RW), col("cb", n, RW),
                                       ALU.mult, ALU.add))
                for k in (1, 2, 3):
                    ins = dve.scalar_tensor_tensor(XC[0:RW, n, k:S], RX[0:RW, n, 0:S - k],
                                                   col("cw", (3 - k) * RB + n, RW), XC[0:RW, n, k:S],
                                                   ALU.mult, ALU.add)
                    if k < 3:
                        link(ins)
                ins.then_inc(sem("conv_done"), 1)

            def flat(b):
                return b[0:RW, :, :].rearrange("p b s -> p (b s)")

            dve.wait_ge(sem("conv_done"), RB)
            dve.wait_ge(sem("rgate_kept"), 2 * RB)
            dve.tensor_tensor(flat(IT), flat(IT), flat(XC), ALU.mult).then_inc(sem("xc_used"), 1)
            dve.wait_ge(sem("xc_used"), 1)
            dve.wait_ge(sem("tanh_done"), RB)
            link(dve.tensor_scalar(flat(RX), flat(RT), 1.0, None, ALU.add))
            link(dve.reciprocal(flat(RX), flat(RX)))
            dve.wait_ge(sem("root_tanh"), 1)
            link(dve.tensor_tensor(flat(XC), flat(XC), flat(RX), ALU.mult))
            link(dve.scalar_tensor_tensor(flat(IT), flat(XC), 2.0, flat(IT), ALU.mult, ALU.mult))
            link(dve.tensor_scalar(flat(RT), flat(RX), 2.0, -1.0, ALU.mult, ALU.add))
            for n in range(RB):
                ins = dve.tensor_tensor_scan(XC[0:RW, n, :], RT[0:RW, n, :], IT[0:RW, n, :], 0.0, ALU.mult, ALU.add)
            link(ins)
            dve.wait_ge(sem("r_kept"), 2 * RB)
            dve.tensor_tensor(flat(XC), flat(XC), flat(RGT), ALU.mult).then_inc(sem("rec_out"), 1)
            dve.wait_ge(sem("rec_out"), 1)
            dve.wait_ge(sem("sq2"), 3 * T)
            link(dve.tensor_reduce(st2[:, 2, :], SQ2.rearrange("p t (h d) -> p (t h) d", d=HD), AX_X, ALU.add))
            dve.tensor_scalar(st2[:, 0, :], st2[:, 2, :], 1.0 / HD, EPS, ALU.mult, ALU.add).then_inc(sem("qk2_meansq"), 1)
            dve.wait_ge(sem("qk2_root"), 1)
            link(dve.reciprocal(st2[:, 2, :], st2[:, 1, :]))
            for t in range(T):
                link(dve.tensor_tensor(N2[:, t, :].rearrange("p (h d) -> p h d", d=HD),
                                       Z2[:, t, 0:D].rearrange("p (h d) -> p h d", d=HD),
                                       bc(st2[:, 2, 24 * t:24 * t + 16], 2, HD), ALU.mult))
            dve.memset(PEB[:, :], 0.0).then_inc(sem("n2_filled"), 1)
            keep_turned("q2", QT2, lambda c: col("gainq"))
            for t in range(T):
                for w, o in enumerate((KS2, KW2)):
                    for dup in range(2):
                        dst = N2[:, t, w * 512:(w + 1) * 512].rearrange("p (g e d) -> p g e d", g=KV, e=2)[:, :, dup, :]
                        link(dve.tensor_tensor(dst, Z2[:, t, o:o + 256].rearrange("p (g d) -> p g d", g=KV),
                                               bc(st2[:, 2, 24 * t + 16 + 4 * w:24 * t + 20 + 4 * w], 2, HD), ALU.mult))
            dve.memset(PEB[:, :], 0.0).then_inc(sem("n2_filled"), 1)
            keep_turned("k2", KT2, lambda c: col("gainkw"))
            for t in range(T):
                for w, o in enumerate((KC2, VC2)):
                    for dup in range(2):
                        dst = N2[:, t, w * 512:(w + 1) * 512].rearrange("p (g e d) -> p g e d", g=KV, e=2)[:, :, dup, :]
                        link(dve.tensor_copy(dst, Z2[:, t, o:o + 256].rearrange("p (g d) -> p g d", g=KV)))
            dve.memset(HID[:, :, :], 0.0).then_inc(sem("n2_filled"), 1)
            for c in range(KC // 2, KC):
                dve.wait_ge(sem("c2_turned"), c // 2 + 1)
                src = PS[:, c // 2, (c % 2) * S:(c % 2 + 1) * S]
                dve.tensor_copy(CT2[0:HD, c, :], src[0:HD, :]).then_inc(sem("c2_kept"), 1)
                dve.tensor_copy(CT2[HD:P, c, 0:S - 1], src[HD:P, 1:S]).then_inc(sem("c2_kept"), 1)
            for i in range(2):
                split_fours("ro", XC, i, f"z{Z2B - 1}", RW)
            wait_used(dve, "cmp")
            dve.wait_ge(sem("n2_filled"), 3)
            dve.tensor_copy(PEB[:, :], PS[:, 2:4, 0:1].rearrange("p a b -> p (a b)")).then_inc(sem("pe_bias"), 1)
            for i in range(2, 4):
                split_fours("ro", XC, i, "", RW)
            dve.wait_ge(sem("cmp_made"), 1)
            link(dve.tensor_copy(kcmp[0:HD, 0, 0:HD], PS[0:HD, 0, 128:128 + HD]))
            link(dve.tensor_copy(vcmp, PS[:, 1, 128:128 + HD]))
            link(dve.tensor_tensor(kcmp[0:HD, 0, HD:P], kcmp[0:HD, 0, 0:HD], kcmp[0:HD, 0, 0:HD], ALU.mult))
            link(dve.tensor_reduce(cst[0:HD, 0, 1:2], kcmp[0:HD, 0, HD:P], AX_X, ALU.add))
            dve.tensor_scalar(cst[0:HD, 0, 0:1], cst[0:HD, 0, 1:2], 1.0 / HD, EPS, ALU.mult,
                              ALU.add).then_inc(sem("kcmp_meansq"), 1)
            dve.wait_ge(sem("kcmp_root"), 1)
            link(dve.reciprocal(cst[0:HD, 0, 2:3], cst[0:HD, 1, 0:1]))
            link(dve.tensor_scalar(kcmp[0:HD, 1, 0:HD], kcmp[0:HD, 0, 0:HD], cst[0:HD, 0, 2:3], None, ALU.mult))
            dve.tensor_scalar(kcmp[0:HD, 1, HD:P], kcmp[0:HD, 0, 0:HD], cst[0:HD, 0, 2:3], None,
                              ALU.mult).then_inc(sem("kcmp_normed"), 1)
            dve.wait_ge(sem("kcmp_turned"), 1)
            dve.tensor_scalar(kcmp[:, 2, 0:HD], PS[:, 2, 0:HD], col("gainkc"), None,
                              ALU.mult).then_inc(sem("kcmp_kept"), 1)
            wait_used(dve, "ro3")
            dve.wait_ge(sem("sig2"), T)
            dve.wait_ge(sem("n3_turned"), KC // 2)
            for t in range(T):
                for half in range(2):
                    o = half * NB
                    dve.tensor_tensor(M2[:, t, o:o + NB], PS[:, 4 + 2 * t + half, :], Z2[:, t, MR2 + o:MR2 + o + NB],
                                      ALU.mult).then_inc(sem("rec_gated"), 1)
            dve.wait_ge(sem("consts2_loaded"), 16)
            dve.wait_ge(sem("cmp_logits"), 1)
            for t in range(T):
                l3 = LC[:, t, :].rearrange("p (h i) -> p h i", h=H2)
                for e in range(2):
                    p3 = PS[:, 3 * e, t * P:(t + 1) * P].rearrange("p (h i) -> p h i", h=H2 // 2)
                    link(dve.scalar_tensor_tensor(l3[:, e:H2:2, :], p3, HD ** -0.5, bc(cneg[:, t, :], 1, H2 // 2),
                                                  ALU.mult, ALU.add))
                link(dve.tensor_reduce(cst[:, 2, t * 16:(t + 1) * 16], l3, AX_X, ALU.max))
                link(dve.tensor_tensor(l3, l3, bc(cst[:, 2, t * 16:(t + 1) * 16], 2, 16), ALU.subtract))
            dve.memset(cst[:, 1, :], 0.0).then_inc(sem("cmp_less_max"), 1)
            dve.wait_ge(sem("c2_turned"), KC // 2)
            link(dve.memset(PZ, 0.0))
            dve.wait_ge(sem("cmp_exp"), 1)
            for t in range(T):
                l3 = LC[:, t, :].rearrange("p (h i) -> p h i", h=H2)
                link(dve.tensor_reduce(cst[:, 2, t * 16:(t + 1) * 16], l3, AX_X, ALU.add))
                link(dve.reciprocal(cst[:, 3, t * 16:(t + 1) * 16], cst[:, 2, t * 16:(t + 1) * 16]))
                link(dve.tensor_tensor(cst[:, 3, t * 16:(t + 1) * 16], cst[:, 3, t * 16:(t + 1) * 16],
                                       NSG[:, t, 0:48:3], ALU.mult))
                link(dve.tensor_tensor(l3, l3, bc(c01[:, t, :], 1, H2), ALU.mult))
                link(dve.tensor_tensor(l3, l3, bc(cst[:, 3, t * 16:(t + 1) * 16], 2, 16), ALU.mult))
                pz = PZ[:, t, :].rearrange("p (h k) -> p h k", h=H2)
                for g in range(KV):
                    link(dve.tensor_copy(pz[:, 4 * g:4 * g + 4, 16 * g:16 * g + 16], l3[:, 4 * g:4 * g + 4, :]))
            dve.memset(cst[:, 1, :], 0.0).then_inc(sem("cmp_probs"), 1)
            keep_turned("pz", PZT)
            attention("a2", HD ** -0.5)
            wait_used(dve, "ao1")
            for t in range(T):
                for half in range(2):
                    o = half * NB
                    link(dve.tensor_tensor(f2[:, half, :], PS[:, 2 * t + half, :], Z2[:, t, MA2 + o:MA2 + o + NB], ALU.mult))
                    dve.tensor_tensor(M2[:, t, o:o + NB], M2[:, t, o:o + NB], f2[:, half, :],
                                      ALU.add).then_inc(sem("m2_ready"), 1)
            keep_turned("m2", MT2)
            for half in range(2):
                wait_used(dve, f"oo{half}")
                for t in range(T):
                    xs = X[:, t, half * NB:(half + 1) * NB]
                    dve.tensor_tensor(xs, xs, PS[:, 4 + 2 * t + half, :], ALU.add).then_inc(sem("x3_ready"), 1)
            dve.wait_ge(sem("x3_ready"), 4)
            scaled("n4", XN4)
            keep_turned("n4", normed2, lambda c: col("n2", c))
            split_input("n4", normed2)
            for f in range(F_B):
                for w, (name, buf) in enumerate((("fg", CG), ("fv", CV))):
                    wait_used(dve, f"{name}{f}")
                    if f == F_B - 1 and w == 1:
                        for i in range(2):
                            split_fours("dn", GV, i, f"fv{f}")
                    for q in range(4):
                        i = w * FT + 4 * f + q
                        src = PS[:, 4 * (f % 2) + 2 * w + q // 2, (q % 2) * S:(q % 2 + 1) * S]
                        if w == 0 and f:
                            dve.wait_ge(sem("ffn_gated"), 4 * (f - 1) + q + 1)
                        link(dve.tensor_scalar(buf[:, q, :], src, col("ffw", 2 * 2 * FT + i), col("ffb", i),
                                               ALU.mult, ALU.add))
                        link(dve.scalar_tensor_tensor(buf[:, q, 1:S], src[:, 0:S - 1], col("ffw", 2 * FT + i),
                                                      buf[:, q, 1:S], ALU.mult, ALU.add))
                        dve.scalar_tensor_tensor(buf[:, q, 2:S], src[:, 0:S - 2], col("ffw", i), buf[:, q, 2:S],
                                                 ALU.mult, ALU.add).then_inc(sem(f"{name}_read"), 1)
                        dve.wait_ge(sem(f"{name}_read"), 4 * f + q + 1)
                        if w == 0:
                            dve.sem_inc(sem("fg_conv"), 1)
                        else:
                            dve.wait_ge(sem("fg_gelu"), 4 * f + q + 1)
                            dve.tensor_tensor(GV[:, 4 * f + q, :], CG[:, q, :], CV[:, q, :],
                                              ALU.mult).then_inc(sem("ffn_gated"), 1)
            dve.wait_ge(sem("ffn_gated"), FT)
            for i in range(2, FT // 4):
                split_fours("dn", GV, i, "")
            wait_used(dve, "dn5")
            for t in range(T):
                for half in range(2):
                    xs = X[:, t, half * NB:(half + 1) * NB]
                    dve.tensor_tensor(xs, xs, PS[:, 2 * t + half, :], ALU.add).then_inc(sem("result_ready"), 1)

        @block.gpsimd
        def _(pool):
            def lower_quarter(b, r=0):
                pool.wait_ge(rounded[b % RING], nth_split(b) + r)
                pool.tensor_tensor(low[:, b % RING, :], ring[:, b % RING, :], high[:, b % RING, :].bitcast(F32),
                                   ALU.subtract).then_inc(left[b % RING], 1)

            first, last = QUARTERS * AT["u0"], QUARTERS * AT["r0"]
            for b in range(QUARTERS * AT["in0"], QUARTERS * AT[f"ada{ADA_DVE}"]):
                if SPLIT[b]:
                    lower_quarter(b)

            n = 0
            for j in range(ADA_DVE, ADA_B):
                for q in range(QUARTERS):
                    wait_loaded(pool, f"ada{j}", q)
                    w = slot(f"ada{j}", q)
                    for c in range(2):
                        dst = ada_acc(j) if q == c == 0 else ada_part[:, c, :]
                        ins = pool.tensor_scalar(dst, w[:, c, :], col("cT", 2 * q + c), None, ALU.mult)
                        if c == 1:
                            free_slot(f"ada{j}", q, ins)
                            wait_used(pool, f"ada{j}", q)
                        else:
                            n += 1
                            ins.then_inc(sem("pool_step"), 1)
                            pool.wait_ge(sem("pool_step"), n)
                        if q or c:
                            n += 1
                            pool.tensor_tensor(ada_acc(j), ada_acc(j), dst, ALU.add).then_inc(sem("pool_step"), 1)
                            pool.wait_ge(sem("pool_step"), n)
            for b in range(QUARTERS * AT["pq0"], first):
                lower_quarter(b)
            with pool.Fori(0, (last - first) // RING) as r:
                for k in range(RING):
                    lower_quarter(first + k, r)
            for b in range(last, N_QUARTERS):
                if SPLIT[b]:
                    lower_quarter(b)


def lay_out(v):
    f = np.float32

    def kblocks(w, cuts):
        k = w.shape[0] // P
        w3 = w.reshape(k, P, w.shape[1])
        res = []
        for idx in cuts:
            blk = np.zeros((P, k, BLK // k), f)
            blk[:, :, :len(idx)] = w3[:, :, idx].transpose(1, 0, 2)
            res.append(blk.reshape(P, BLK))
        return res

    def column_quarters(w, cuts):
        w3 = w.reshape(KC, P, w.shape[1])
        qs = np.zeros((len(cuts), P, KC, P), f)
        for i, idx in enumerate(cuts):
            qs[i, :, :, :len(idx)] = w3[:, :, idx].transpose(1, 0, 2)
        return list(qs.reshape(len(cuts) // QUARTERS, QUARTERS, P, QUARTER))

    def ranges(n, w=NB):
        return [np.arange(i, min(i + w, n)) for i in range(0, n, w)]

    def rows4(w):
        k = w.shape[0] // P
        return [w.reshape(k, P, D)[4 * i:4 * i + 4].transpose(1, 0, 2).reshape(P, BLK) for i in range(k // 4)]

    blocks = {}

    def put(prefix, lst):
        for i, b in enumerate(lst):
            blocks[f"{prefix}{i}"] = b

    put("ada", kblocks(v["w_ada"][0], ranges(6 * D)))
    put("in", kblocks(v["w_in"][0], ranges(Z1W)))
    blocks["up_attn"] = rows4(v["w_up_attn"][0])[0]
    blocks["up_pool"] = rows4(v["w_up_pool"][0])[0]
    put("out", kblocks(v["w_out"][0], ranges(D)))
    put("pq", column_quarters(v["w_peer_q"][0], ranges(D, P)))
    w2 = v["w_in_2"]
    rnn = 2 * RB * RW
    nsa = rnn + H2 * HD + 6 * KV * HD
    groups = ranges(rnn, RW)
    for k in range(2):
        groups[k - 2] = np.concatenate([groups[k - 2], np.arange(nsa + k * GATES // 2, nsa + (k + 1) * GATES // 2)])
    put("r", column_quarters(w2, groups))
    rest = np.concatenate([np.arange(rnn, nsa), np.arange(nsa + 48, w2.shape[1])])
    put("z", kblocks(w2, [rest[i] for i in ranges(Z2W)]))
    rg = np.zeros((P, BLK), f)
    for i, w in enumerate((v["rg_w_a_2"], v["rg_w_x_2"])):
        for k in range(2):
            o = (2 * i + k) * QUARTER
            rg[:RW, o:o + RB // 2 * RW] = w[8 * k:8 * k + 8].transpose(1, 0, 2).reshape(RW, -1)
    blocks["rgate"] = rg
    cmp_w = np.stack([v["cmp_w1_k_2"], v["cmp_w1_v_2"]]).reshape(2, CLEN // 2, P, P)
    blocks["cmp"] = cmp_w.transpose(2, 0, 1, 3).reshape(P, BLK)
    ro = np.zeros((4, P, 4, D), f)
    ro[:, :RW] = v["w_rnn_out_2"].reshape(4, 4, RW, D).transpose(0, 2, 1, 3)
    put("ro", list(ro.reshape(4, P, BLK)))
    put("ao", kblocks(v["w_attn_out_2"], ranges(D)))
    put("oo", kblocks(v["w_out_2"], ranges(D)))
    put("fg", column_quarters(v["w_up_2"][:, :FF], ranges(FF, P)))
    put("fv", column_quarters(v["w_up_2"][:, FF:], ranges(FF, P)))
    put("dn", rows4(v["w_down_2"]))
    stream = np.empty((len(ORDER), QUARTERS, P, QUARTER), f)
    quarters = stream.reshape(N_QUARTERS, P, QUARTER)
    for n, b in blocks.items():
        for q, part in enumerate(b if b.ndim == 3 else b.reshape(P, QUARTERS, QUARTER).transpose(1, 0, 2)):
            quarters[quarter_no(n, q)] = part
    u = v["peer_u"][0].reshape(NK, U_BLOCKS, QUARTERS, KC, P)
    stream[AT["u0"]:AT["u0"] + U_BLOCKS] = u.transpose(1, 2, 4, 3, 0).reshape(U_BLOCKS, QUARTERS, P, QUARTER)
    vv = v["peer_v"][0].reshape(NK, U_BLOCKS, QUARTERS, QUARTER)
    stream[AT["v0"]:AT["v0"] + U_BLOCKS] = vv.transpose(1, 2, 0, 3)

    cols = np.zeros((P, NCOL), f)

    def place(name, m):
        o = COL[name][0]
        assert m.shape[1] == COL[name][1], name
        cols[:m.shape[0], o:o + m.shape[1]] = m

    def feat(x):
        return x.reshape(-1, P).T

    twice = lambda x: np.concatenate([x, x])[:, None]
    place("cT", feat(v["c"][0]))
    place("g1", feat(v["g_norm1"][0]))
    place("g2", feat(v["g_norm2"][0]))
    place("bada", feat(v["b_ada"][0]))
    gq, gk, gi = twice(v["g_q"][0]), twice(v["g_k"][0]), twice(v["g_ik"][0])
    one = np.ones((P, 1), f)
    place("gain1", np.concatenate([gq] * 4 + [gk, one, one, gi], axis=1))
    place("spool", v["s_pool"][0].T)
    place("n1", feat(v["norm1_g_2"]))
    place("n2", feat(v["norm2_g_2"]))
    place("gainq", twice(v["q_norm_g_2"]))
    place("gainks", twice(v["k_slc_norm_g_2"]))
    place("gainkw", twice(v["k_win_norm_g_2"]))
    place("gainkc", twice(v["k_cmp_norm_g_2"]))
    place("pek", v["cmp_pe_k_2"].reshape(CLEN // 2, P).T)
    place("pev", v["cmp_pe_v_2"].reshape(CLEN // 2, P).T)
    place("ffw", np.concatenate([feat(v["ffn_conv_w_2"][k]) for k in range(3)], axis=1))
    place("ffb", feat(v["ffn_conv_b_2"]))
    place("ba", v["rg_b_a_2"].reshape(RB, RW).T)
    place("bx", v["rg_b_x_2"].reshape(RB, RW).T)
    place("lam", v["lru_lambda_2"].reshape(RB, RW).T)
    place("cw", np.concatenate([v["rnn_conv_w_2"][k].reshape(RB, RW).T for k in range(4)], axis=1))
    place("cb", v["rnn_conv_b_2"].reshape(RB, RW).T)

    consts = np.concatenate([np.eye(P), np.tile(np.arange(P), (P, 1)), np.ones((P, P))], axis=1).astype(f)
    s, t = np.arange(S)[:, None], np.arange(S)[None, :]
    band = np.stack([((s <= t) & (s > t - w)) / np.minimum(t + 1, w) - (s == t) for w in (2, 4, 8, 16)])
    band = band.reshape(4, T, P, S).transpose(2, 1, 0, 3).reshape(P, -1).astype(f)
    q = np.arange(S)
    causal = np.where(np.arange(S)[None] <= q[:, None], 0.0, MASKED).reshape(T, P, S).transpose(1, 0, 2).reshape(P, -1)
    i = np.arange(16)
    ok = (i[None] < NCMP) & (i[None] * CSTEP + CLEN - 1 <= q[:, None])
    ok = ok.reshape(T, P, 16).transpose(1, 0, 2).reshape(P, -1)
    consts2 = np.concatenate([causal.astype(f), np.where(ok, 0.0, MASKED).astype(f), ok.astype(f),
                              v["cmp_w2_k_2"], v["cmp_w2_v_2"]], axis=1)
    return {
        "x": v["x"][0], "stream": stream, "cols": cols, "consts": consts, "consts2": consts2, "band": band,
        "brow": v["b_ada"][0][None, 2 * D:3 * D], "wpool": v["w_pool_grp"][0].transpose(1, 0, 2).reshape(P, -1),
        "skeys": v["peer_subkeys"][0].transpose(1, 3, 0, 2).reshape(P, -1),
    }


def kernel(**inputs):
    import concourse.bacc as _bacc
    from concourse.bass_utils import run_bass_kernel_spmd as _run

    nc = _bacc.Bacc("TRN2", target_bir_lowering=False, num_devices=1)
    arrays = {n: np.ascontiguousarray(x) for n, x in lay_out({k: np.asarray(x) for k, x in inputs.items()}).items()}
    aps = {n: nc.dram_tensor(f"in_{n}", x.shape, mybir.dt.from_np(x.dtype), kind="ExternalInput").ap()
           for n, x in arrays.items()}
    out = nc.dram_tensor("result", (S, D), F32, kind="ExternalOutput").ap()
    build_program(nc, aps, out)
    r = _run(nc, [{f"in_{n}": x for n, x in arrays.items()}], core_ids=[0])
    return r.results[0]["result"].reshape(1, S, D)
```
